# Optimizing a Trainium2 kernel written in Bass

```python
import jax, jax.numpy as jnp
from jax import lax
import numpy as np

D_MODEL = 1024
BATCH = 1
SEQ = 1024
DEPTH = 1
DEC_BATCH = 8
DEC_SEQ = 1
PAST_LEN = 8192
PAGE_SIZE = 128

EPS = 1e-6
POOL_GROUPS = 4
POOL_IN = D_MODEL // 2
POOL_GC = POOL_IN // POOL_GROUPS
POOL_OUT_GC = D_MODEL // POOL_GROUPS
POOL_WINDOWS = (2, 4, 8, 16)
POOL_HIST = max(POOL_WINDOWS) - 1
RET_HEADS = 4
RET_DK = D_MODEL // 8
RET_DV = D_MODEL // RET_HEADS
RET_CHUNK = 128
ROPE_BASE = 10000.0
N_GROUPS = 4
EXPERTS_PER_GROUP = 8
N_EXPERTS = N_GROUPS * EXPERTS_PER_GROUP
TOP_K_EXPERT = 2
D_EXPERT = D_MODEL // 4
MOE_BLOCK = 128
QK_W = RET_HEADS * RET_DK
V_W = RET_HEADS * RET_DV
IN_SPLITS = (POOL_IN, POOL_IN + QK_W, POOL_IN + 2 * QK_W, POOL_IN + 2 * QK_W + V_W, POOL_IN + 2 * QK_W + V_W + D_MODEL)
IN_WIDTH = POOL_IN + 2 * QK_W + V_W + 2 * D_MODEL

kernel_name = 'hybrid_pool_retention_hmoe_step'

def rmsnorm(x, g):
    xf = x.astype(jnp.float32)
    inv = lax.rsqrt(jnp.mean(xf * xf, axis=-1, keepdims=True) + EPS)
    return (xf * inv * g.astype(jnp.float32)).astype(x.dtype)

def rotary(x, pos):
    half = x.shape[-1] // 2
    freqs = ROPE_BASE ** (-jnp.arange(half, dtype=jnp.float32) / half)
    ang = pos[:, None] * freqs[None, :]
    cos = jnp.cos(ang)[None, :, None, :]
    sin = jnp.sin(ang)[None, :, None, :]
    x1, x2 = x[..., :half], x[..., half:]
    return jnp.concatenate([x1 * cos - x2 * sin, x1 * sin + x2 * cos], axis=-1)

def pool_mixer(u, hist, hist_valid, w_pool, pool_scale):
    B, L, _ = u.shape
    full = jnp.concatenate([hist.astype(u.dtype), u], axis=1)
    valid = jnp.concatenate([hist_valid.astype(jnp.float32), jnp.ones((L,), jnp.float32)])
    cs = jnp.pad(jnp.cumsum(full.astype(jnp.float32), axis=1), ((0, 0), (1, 0), (0, 0)))
    cv = jnp.pad(jnp.cumsum(valid), (1, 0))
    hi = POOL_HIST + 1
    groups = []
    for g, w in enumerate(POOL_WINDOWS):
        sl = slice(g * POOL_GC, (g + 1) * POOL_GC)
        s = cs[:, hi:hi + L, sl] - cs[:, hi - w:hi - w + L, sl]
        n = cv[hi:hi + L] - cv[hi - w:hi - w + L]
        groups.append(s / n[None, :, None] - u[:, :, sl].astype(jnp.float32))
    pooled = jnp.stack(groups, axis=2)
    out = jnp.einsum('blgc,gcd->blgd', pooled, w_pool.astype(jnp.float32)).reshape(B, L, D_MODEL)
    out = out * pool_scale.astype(jnp.float32)
    new_hist = full[:, -POOL_HIST:]
    return out, new_hist

def retention(q, k, v, s0):
    B, L, H, _ = q.shape
    C = RET_CHUNK if L % RET_CHUNK == 0 else L
    n = L // C
    log_g = jnp.log(1.0 - jnp.exp2(-5.0 - jnp.arange(H, dtype=jnp.float32)))
    i = jnp.arange(C, dtype=jnp.float32)
    diff = i[:, None] - i[None, :]
    dmask = jnp.where(diff >= 0, jnp.exp(jnp.maximum(diff, 0.0)[None] * log_g[:, None, None]), 0.0)
    xi = jnp.exp((i[:, None] + 1.0) * log_g[None, :])
    zeta = jnp.exp((C - 1.0 - i)[:, None] * log_g[None, :])
    g_chunk = jnp.exp(C * log_g)

    def to_chunks(a):
        return jnp.moveaxis(a.reshape((B, n, C) + a.shape[2:]), 1, 0)

    def step(s, qkv):
        qc, kc, vc = qkv
        scores = jnp.einsum('bihk,bjhk->bhij', qc, kc) * dmask[None]
        o = (jnp.einsum('bhij,bjhv->bihv', scores, vc)
             + jnp.einsum('bihk,bhkv->bihv', qc, s) * xi[None, :, :, None])
        s = g_chunk[None, :, None, None] * s + jnp.einsum('bjhk,bjhv->bhkv', kc * zeta[None, :, :, None], vc)
        return s, o

    s_new, o = lax.scan(step, s0, (to_chunks(q), to_chunks(k), to_chunks(v)))
    o = jnp.moveaxis(o, 0, 1).reshape(B, L, H, v.shape[-1])
    return o, s_new

def head_group_norm(o, gain):
    B, L, H, DV = o.shape
    mu = jnp.mean(o, axis=-1, keepdims=True)
    var = jnp.mean(jnp.square(o - mu), axis=-1, keepdims=True)
    o = (o - mu) * lax.rsqrt(var + EPS)
    return o.reshape(B, L, H * DV) * gain.astype(jnp.float32)

def hier_moe(h, w_grp, w_exp, w1, w3, w2):
    T, D = h.shape
    logits_g = jnp.einsum('td,dg->tg', h, w_grp).astype(jnp.float32)
    p_grp = jax.nn.softmax(logits_g, axis=-1)
    g_idx = jnp.argmax(logits_g, axis=-1)
    p_g = jnp.take_along_axis(p_grp, g_idx[:, None], axis=1)[:, 0]
    logits_e = jnp.einsum('td,dge->tge', h, w_exp).astype(jnp.float32)
    le = jnp.take_along_axis(logits_e, g_idx[:, None, None], axis=1)[:, 0]
    top_v, top_i = lax.top_k(le, TOP_K_EXPERT)
    p_e = jax.nn.softmax(top_v, axis=-1)
    expert = g_idx[:, None] * EXPERTS_PER_GROUP + top_i
    weight = p_g[:, None] * p_e
    A = T * TOP_K_EXPERT
    a_exp = expert.reshape(A).astype(jnp.int32)
    a_w = weight.reshape(A)
    a_tok = jnp.repeat(jnp.arange(T, dtype=jnp.int32), TOP_K_EXPERT)
    order = jnp.argsort(a_exp)
    s_exp, s_tok, s_w = a_exp[order], a_tok[order], a_w[order]
    counts = jnp.bincount(a_exp, length=N_EXPERTS)
    padded = ((counts + MOE_BLOCK - 1) // MOE_BLOCK) * MOE_BLOCK
    pad_end = jnp.cumsum(padded)
    pad_start = pad_end - padded
    start = jnp.cumsum(counts) - counts
    slot = pad_start[s_exp] + (jnp.arange(A, dtype=jnp.int32) - start[s_exp])
    n_blocks = -(-A // MOE_BLOCK) + N_EXPERTS
    n_slots = n_blocks * MOE_BLOCK
    slot_tok = jnp.zeros((n_slots,), jnp.int32).at[slot].set(s_tok)
    slot_w = jnp.zeros((n_slots,), jnp.float32).at[slot].set(s_w)
    block_exp = jnp.minimum(jnp.searchsorted(pad_end, jnp.arange(n_blocks) * MOE_BLOCK, side='right'), N_EXPERTS - 1)

    def run_block(args):
        tok, w, e = args
        xb = h[tok]
        a = jax.nn.silu(xb @ w1[e]) * (xb @ w3[e])
        return ((a @ w2[e]).astype(jnp.float32) * w[:, None]).astype(h.dtype)

    out_blocks = lax.map(run_block, (slot_tok.reshape(n_blocks, MOE_BLOCK), slot_w.reshape(n_blocks, MOE_BLOCK), block_exp))
    return jax.ops.segment_sum(out_blocks.reshape(n_slots, D), slot_tok, num_segments=T)

def layer(x, pool_hist, pool_valid, ret_state, pos0, g_mix, w_in, w_pool, pool_scale, ret_gn, w_out, g_ffn, w_grp, w_exp, w1, w3, w2):
    B, L, _ = x.shape
    h = rmsnorm(x, g_mix)
    z = h @ w_in
    u, q, k, v, ga, gb = jnp.split(z, IN_SPLITS, axis=-1)
    pool_out, new_hist = pool_mixer(u, pool_hist, pool_valid, w_pool, pool_scale)
    pos = (pos0 + jnp.arange(L)).astype(jnp.float32)
    qf = rotary(q.astype(jnp.float32).reshape(B, L, RET_HEADS, RET_DK), pos)
    kf = rotary(k.astype(jnp.float32).reshape(B, L, RET_HEADS, RET_DK), pos) * (RET_DK ** -0.5)
    vf = v.astype(jnp.float32).reshape(B, L, RET_HEADS, RET_DV)
    ret, s_new = retention(qf, kf, vf, ret_state.astype(jnp.float32))
    ret_out = head_group_norm(ret, ret_gn)
    mixed = (jax.nn.sigmoid(ga.astype(jnp.float32)) * pool_out
             + jax.nn.sigmoid(gb.astype(jnp.float32)) * ret_out).astype(x.dtype)
    x = x + mixed @ w_out
    h2 = rmsnorm(x, g_ffn).reshape(B * L, D_MODEL)
    x = x + hier_moe(h2, w_grp, w_exp, w1, w3, w2).reshape(B, L, D_MODEL)
    return x, new_hist, s_new

def setup_inputs(seed: int = 0) -> dict:
    key = jax.random.key(seed)
    ks = jax.random.split(key, 18)

    def nrm(k, shape, scale):
        return jax.random.normal(k, shape, jnp.float32) * scale

    return {
        'x_prompt': nrm(ks[0], (BATCH, SEQ, D_MODEL), 1.0),
        'x_sample': nrm(ks[1], (DEC_BATCH, DEC_SEQ, D_MODEL), 1.0),
        'state_pool': nrm(ks[2], (DEPTH, DEC_BATCH, POOL_HIST, POOL_IN), 1.0),
        'state_ret': nrm(ks[3], (DEPTH, DEC_BATCH, RET_HEADS, RET_DK, RET_DV), 0.5),
        'g_mix': 1.0 + nrm(ks[4], (DEPTH, D_MODEL), 0.05),
        'w_in': nrm(ks[5], (DEPTH, D_MODEL, IN_WIDTH), D_MODEL ** -0.5),
        'w_pool': nrm(ks[6], (DEPTH, POOL_GROUPS, POOL_GC, POOL_OUT_GC), POOL_GC ** -0.5),
        'pool_scale': 1.0 + nrm(ks[7], (DEPTH, D_MODEL), 0.1),
        'ret_gn': 1.0 + nrm(ks[8], (DEPTH, D_MODEL), 0.05),
        'w_out': nrm(ks[9], (DEPTH, D_MODEL, D_MODEL), D_MODEL ** -0.5),
        'g_ffn': 1.0 + nrm(ks[10], (DEPTH, D_MODEL), 0.05),
        'w_grp': nrm(ks[11], (DEPTH, D_MODEL, N_GROUPS), D_MODEL ** -0.5),
        'w_exp': nrm(ks[12], (DEPTH, D_MODEL, N_GROUPS, EXPERTS_PER_GROUP), D_MODEL ** -0.5),
        'w1': nrm(ks[13], (DEPTH, N_EXPERTS, D_MODEL, D_EXPERT), D_MODEL ** -0.5),
        'w3': nrm(ks[14], (DEPTH, N_EXPERTS, D_MODEL, D_EXPERT), D_MODEL ** -0.5),
        'w2': nrm(ks[15], (DEPTH, N_EXPERTS, D_EXPERT, D_MODEL), D_EXPERT ** -0.5),
        'g_final': 1.0 + nrm(ks[16], (D_MODEL,), 0.05),
    }

def reference(x_prompt, x_sample, state_pool, state_ret, g_mix, w_in, w_pool, pool_scale, ret_gn, w_out, g_ffn, w_grp, w_exp, w1, w3, w2, g_final):
    bp = x_prompt.shape[0]
    yp, ys = x_prompt, x_sample
    pool_p, ret_p, pool_s, ret_s = [], [], [], []
    for l in range(DEPTH):
        params = (g_mix[l], w_in[l], w_pool[l], pool_scale[l], ret_gn[l], w_out[l], g_ffn[l], w_grp[l], w_exp[l], w1[l], w3[l], w2[l])
        yp, hp, sp = layer(yp, jnp.zeros((bp, POOL_HIST, POOL_IN), yp.dtype), jnp.zeros((POOL_HIST,), jnp.float32),
                           jnp.zeros((bp, RET_HEADS, RET_DK, RET_DV), jnp.float32), 0, *params)
        ys, hs, ss = layer(ys, state_pool[l], jnp.ones((POOL_HIST,), jnp.float32), state_ret[l], PAST_LEN, *params)
        pool_p.append(hp)
        ret_p.append(sp)
        pool_s.append(hs)
        ret_s.append(ss)
    y_prompt = rmsnorm(yp, g_final)
    y_sample = rmsnorm(ys, g_final)
    new_pool_prompt = jnp.stack(pool_p, axis=0)
    new_ret_prompt = jnp.stack(ret_p, axis=0)
    new_pool_sample = jnp.stack(pool_s, axis=0)
    new_ret_sample = jnp.stack(ret_s, axis=0)
    return (y_prompt, y_sample, new_pool_prompt, new_ret_prompt, new_pool_sample, new_ret_sample)


_drawn_inputs = setup_inputs


def setup_inputs(seed=0):
    import zlib

    import numpy as np

    out = dict(_drawn_inputs(seed))
    spreads = {}
    factors = {}
    for name, (base, spread) in spreads.items():
        noise = np.random.default_rng([zlib.crc32(name.encode()), seed]).standard_normal(out[name].shape)
        drawn = base * np.exp(spread * noise) if base else spread * noise
        out[name] = __import__('jax').numpy.asarray(drawn.astype(out[name].dtype))
    for name, factor in factors.items():
        out[name] = (out[name] * factor).astype(out[name].dtype)
    return out
```

```python
from contextlib import ExitStack

import numpy as np

import concourse.bass as bass
from concourse import mybir

F32 = mybir.dt.float32
F32R = mybir.dt.float32r
I32 = mybir.dt.int32
ALU = mybir.AluOpType
ACT = mybir.ActivationFunctionType
AX = mybir.AxisListType.X

P = 128
D = 1024
KT = D // P
SEQ, NB, NTOK = 1024, 8, 1032
NT = 9
CH = SEQ // P
TC = NTOK // 3
H = 4
DV = 256
EPS = 1e-6
HIST = 15
SPAN = HIST + SEQ + 16 * NB
LAST = NTOK - P
Q3 = 96
NE, EPG, FE = 32, 8, 256
SPILL = 16
NBLK = NE + SPILL
SLOTS = 4
MAGIC = float(0x5F3759DF)
PAST = 8192
HCW = 2 * P + 16 + 8


def shape_constants():
    half = P // 2
    freqs = (10000.0 ** (-np.arange(half, dtype=np.float64) / half)).astype(np.float32)
    pos = np.concatenate([np.arange(SEQ), np.full(NB, PAST)]).astype(np.float32)
    ang = (pos[:, None] * freqs[None, :]).astype(np.float32).astype(np.float64)
    cs = np.zeros((P, 2, NTOK), np.float32)
    cs[:half, 0] = cs[half:, 0] = np.cos(ang).T
    cs[:half, 1] = np.sin(ang).T
    cs[half:, 1] = -np.sin(ang).T
    log_g = np.log(1.0 - 2.0 ** (-5.0 - np.arange(H)))
    i = np.arange(P)
    scale = P ** -0.5
    hc = np.zeros((P, H, HCW), np.float32)
    for h in range(H):
        d = i[None, :] - i[:, None]
        hc[:, h, 0:P] = np.where(d >= 0, np.exp(np.maximum(d, 0) * log_g[h]), 0.0) * scale
        hc[:, h, P:2 * P] = np.exp((i + 1.0) * log_g[h])[None, :]
        w = 2 << h
        hc[:, h, 2 * P:2 * P + 16] = (w / np.minimum(np.arange(16) + 1, w))[None, :]
        o = 2 * P + 16
        hc[:, h, o + 0] = np.exp((P - 1.0 - i) * log_g[h]) * scale
        hc[:, h, o + 1] = np.exp(P * log_g[h])
        hc[:, h, o + 2] = np.exp(log_g[h])
        hc[:, h, o + 3] = 1.0 / w
        for level in range(1, 4):
            hc[:, h, o + 3 + level] = float(w > (1 << level))
    m = np.zeros((P, MISC), np.float32)
    m[:, IDENT:IDENT + P] = np.eye(P)
    m[:, BEFORE:BEFORE + P] = i[:, None] < i[None, :]
    m[:, ONES:ONES + P] = 1.0
    m[:, IOTA:IOTA + P] = i[None, :]
    m[:, REV:REV + 8] = 8 - np.arange(8)[None, :]
    m[:, THR:THR + 8] = 128.0 * (np.arange(8)[None, :] + 1)
    tok = np.arange(NT)[None, :] * P + i[:, None]
    m[:, AID:AID + 2 * NT] = (2 * tok[:, :, None] + np.arange(2)).reshape(P, 2 * NT)
    m[:, TOKC:TOKC + 2 * NT] = np.repeat(tok, 2, axis=1)
    m[:, LIVE:LIVE + 2 * NT] = np.repeat(tok < NTOK, 2, axis=1)
    m[:, QMASK:QMASK + NB * 32] = (np.arange(32)[None, :] == 24 + np.arange(NB)[:, None]).reshape(1, -1)
    m[:, KMASK:KMASK + NB] = i[:, None] == 120 + np.arange(NB)[None, :]
    return cs, hc, m


IDENT, BEFORE, ONES, IOTA = 0, P, 2 * P, 3 * P
REV = 4 * P
THR = REV + 8
AID = THR + 8
LIVE = AID + 2 * NT
TOKC = LIVE + 2 * NT
QMASK = TOKC + 2 * NT
KMASK = QMASK + NB * 32
MISC = KMASK + NB


class Region:

    def __init__(self, nc, start, size):
        self.nc, self.at, self.end, self.where = nc, start, start + size, {}

    def place(self, name, shape, dtype):
        t = self.nc.alloc_sbuf_tensor_at(name, list(shape), dtype, offset=self.at)
        self.where[name] = self.at
        self.at += -(-int(np.prod(shape[1:])) * 4 // 32) * 32
        assert self.at <= self.end, (name, self.at - self.end)
        return t


class Steps:

    def __init__(self, eng, sem, carrier=None):
        self.eng, self.sem, self.carrier, self.base, self.n = eng, sem, carrier, 0, 0

    def do(self, ins):
        ins.then_inc(self.sem, 1)
        self.n += 1
        self.eng.wait_ge(self.sem, self.base + self.n)
        if self.carrier is not None:
            self.eng.sem_inc(self.carrier, 1)

    def round_(self, start, index, per):
        self.base, self.n = start + index * per, 0


def newton_rsqrt(steps, eng, x, y, half, t, rounds=3):
    steps.do(eng.tensor_scalar(half, x, -0.5, None, ALU.mult))
    for r in range(rounds):
        steps.do(eng.tensor_tensor(t, y, y, ALU.mult))
        steps.do(eng.tensor_tensor(t, t, half, ALU.mult))
        steps.do(eng.tensor_scalar(t, t, 1.5, None, ALU.add))
        last = eng.tensor_tensor(y, y, t, ALU.mult)
        if r < rounds - 1:
            steps.do(last)
    return last


NEWTON = 12


def rsqrt_guess(steps, eng, x, y, shifted):
    steps.do(eng.tensor_scalar(shifted, x.bitcast(I32), 1, None, ALU.logical_shift_right))
    return eng.tensor_scalar(y.bitcast(I32), shifted, -1.0, MAGIC, ALU.mult, ALU.add)


def step_kernel(nc, x_prompt, x_sample, state_pool, state_ret, g_mix, w_in, w_pool, pool_scale, ret_gn,
                w_out, g_ffn, w_grp, w_exp, w1, w3, w2, g_final, c_cs, c_hc, c_misc,
                y_prompt, y_sample, pool_p, ret_p, pool_s, ret_s):
    w_in = w_in[0].rearrange("(k p) n -> p k n", p=P)
    w_out = w_out[0].rearrange("(k p) n -> p k n", p=P)
    x_p = x_prompt[0]
    x_s = x_sample.rearrange("b o d -> (b o) d")
    mixed_d = nc.dram_tensor("mixed_d", [NTOK, D], F32).ap()
    h2_d = nc.dram_tensor("h2_d", [NTOK, D], F32).ap()
    part_d = nc.dram_tensor("part_d", [2 * NTOK, D], F32).ap()

    with ExitStack() as ctx:
        def sem(name):
            return ctx.enter_context(nc.semaphore(name))

        banks = [ctx.enter_context(nc.psum_tensor(f"bank{i}", [P, 512], F32)) for i in range(8)]

        base = -(-nc.sbuf_base // 32) * 32
        size = (nc.sbuf_top - base) // 32 * 32
        ctx.enter_context(nc.sbuf_tensor("arena", [P, size // 4], F32))
        whole = Region(nc, base, size)
        misc = whole.place("misc", [P, MISC], F32)
        small = whole.place("small", [P, 96], F32)
        bits = whole.place("bits", [P, 32], I32)
        at_hT = whole.at
        hT = [whole.place(n, [P, KT, NTOK], F32R) for n in ("hT_hi", "hT_lo")]
        at_W = whole.at
        wuqk = [whole.place(n, [P, 3, KT, P], F32R) for n in ("wuqk_hi", "wuqk_lo")]
        at_vg = whole.at
        wvg = [whole.place(n, [P, 3, KT, DV], F32R) for n in ("wvg_hi", "wvg_lo")]
        raw = [whole.place(f"raw{i}", [P, 512], F32) for i in range(3)]
        at_small = whole.at

        ra = Region(nc, at_vg, 2 * 3 * KT * DV * 4)
        xall = ra.place("xall", [P, NT, D], F32)
        gmix_b = ra.place("gmix_b", [P, D], F32)
        junk_a = ra.place("junk_a", [P, D], F32)

        rb = Region(nc, at_small, whole.end - at_small)
        cs = rb.place("cs", [P, 2, NTOK], F32)
        hc = rb.place("hc", [P, H, HCW], F32)
        gn_b = rb.place("gn_b", [P, D], F32)
        line = [rb.place(f"line{i}", [P, SPAN + 1], F32) for i in range(3)]
        qT = rb.place("qT", [P, NTOK], F32)
        kT = rb.place("kT", [P, NTOK], F32)
        qx = [rb.place(f"qx{i}", [P, P], F32) for i in range(2)]
        state = rb.place("state", [P, DV], F32)
        sst = [rb.place(f"sample_state{i}", [P, 2, DV], F32) for i in range(2)]
        wp_raw = rb.place("wp_raw", [P, DV], F32)
        wp = rb.place("wp", [P, DV], F32)
        ps_b = rb.place("ps_b", [P, DV], F32)
        vb = [rb.place(f"v{i}", [P, DV], F32) for i in range(2)]
        sg = [rb.place(f"sg{i}", [P, 2 * DV], F32) for i in range(2)]
        sgn = [t[:, DV:2 * DV] for t in sg]
        kz = [rb.place(f"kz{i}", [P, P], F32) for i in range(2)]
        scm = [rb.place(f"scm{i}", [P, P], F32) for i in range(2)]
        onorm = rb.place("onorm", [P, DV], F32)
        pgate = rb.place("pgate", [P, DV], F32)
        mixed = [rb.place(f"mixed{i}", [P, DV], F32) for i in range(2)]
        uout = rb.place("uout", [P, 2, P], F32)
        qm = rb.place("qm", [P, NB, 32], F32)
        ps32 = rb.place("ps32", [P, 32], F32)
        hist = nc.alloc_sbuf_tensor_at("hist", [P, P], F32, offset=rb.where["scm1"])
        kblk = nc.alloc_sbuf_tensor_at("kblk", [P, NB, P], F32, offset=rb.where["line2"])
        rot = nc.alloc_sbuf_tensor_at("rot", [P, TC], F32, offset=rb.where["line2"])

        rh = Region(nc, at_hT, 2 * KT * NTOK * 4)
        x2 = rh.place("x2", [P, NT, D], F32)
        at_rest = rh.at
        mT = [[rh.place(f"mT_{n}{i}", [P, KT, P], F32R) for n in ("hi", "lo")] for i in range(2)]
        mi = [rh.place(f"mixed_in{i}", [P, D], F32) for i in range(2)]
        rw = Region(nc, at_W, 2 * 3 * KT * (P + DV) * 4)
        wo = [[rw.place(f"wo_{n}{k}", [P, D], F32R) for n in ("hi", "lo")] for k in range(KT)]
        wo_raw = [nc.alloc_sbuf_tensor_at(f"wo_raw{k}", [P, D], F32, offset=rw.where[f"wo_lo{k}"])
                  for k in range(3, KT)]
        rc = Region(nc, at_small, whole.end - at_small)
        xr = [rc.place(f"x_again{i}", [P, D], F32) for i in range(2)]
        h2 = [rc.place(f"h2_{i}", [P, D], F32) for i in range(2)]
        h2T = [rc.place(f"h2T{i}", [P, KT, P], F32) for i in range(2)]
        junk_c = rc.place("junk_c", [P, D], F32)
        gffn_b = rc.place("gffn_b", [P, D], F32)
        wr = rc.place("w_router", [P, KT, 36], F32)

        logits = rc.place("logits", [P, NT, 36], F32)
        tmp_e = rc.place("tmp_e", [P, 2 * NT, NE], F32)
        chosen = rc.place("chosen", [P, 2 * NT, NE], F32)
        both = rc.place("both", [P, NT, NE], F32)
        before_e = rc.place("before_e", [P, NT + 1, NE], F32)
        vec = rc.place("vec", [P, 16, 2 * NT], F32)
        evec = rc.place("evec", [P, 4, NE], F32)
        pair_w = rc.place("pair_w", [P, NT, 2], F32)
        idx_tok = rc.place("idx_tok", [P, NBLK], I32)
        idx_pair = rc.place("idx_pair", [P, NBLK], I32)
        spill = rc.place("spill", [P, 2 * SPILL + 1], I32)
        icol = [rc.place(f"icol{i}", [P, 1], I32) for i in range(SLOTS)]
        jcol = [rc.place(f"jcol{i}", [P, 1], I32) for i in range(SLOTS)]
        rt = Region(nc, at_rest, at_hT + 2 * KT * NTOK * 4 - at_rest)
        slot_hot = rt.place("slot_hot", [P, 2 * NT, P], F32)
        planes = rt.place("planes", [P, 2 * NT, 3 * NBLK], F32)

        rm = Region(nc, at_W, 2 * 3 * KT * (P + DV) * 4)
        w13, w2t = [], []
        for i in range(SLOTS):
            r = rm if i < 3 else Region(nc, at_rest, at_hT + 2 * KT * NTOK * 4 - at_rest)
            w13.append(r.place(f"w13_{i}", [P, 2, KT, FE], F32))
            w2t.append(r.place(f"w2_{i}", [P, 2, D], F32))
        rx = Region(nc, at_small, whole.end - at_small)
        xg = [rx.place(f"xg{i}", [P, D], F32) for i in range(SLOTS)]
        xT = [rx.place(f"xT{i}", [P, KT, P], F32) for i in range(2)]
        yb = [rx.place(f"y{i}", [P, D], F32) for i in range(2)]
        sig = [rx.place(f"sig{i}", [P, FE], F32) for i in range(2)]
        act1 = rx.place("act1", [P, FE], F32)
        aa = [rx.place(f"a{i}", [P, FE], F32) for i in range(2)]
        aT = [rx.place(f"aT{i}", [P, 2, P], F32) for i in range(2)]
        assert rx.at <= rc.where["vec"]

        rf = Region(nc, at_W, 2 * 3 * KT * (P + DV) * 4)
        parts = [rf.place(f"parts{i}", [P, 2, D], F32) for i in range(3)]
        zt = [rf.place(f"z{i}", [P, D], F32) for i in range(3)]
        gfin_b = rf.place("gfin_b", [P, D], F32)
        junk_f = rf.place("junk_f", [P, D], F32)

        SS, MS, RS = 0, 9, 18
        HX, TX = 27, 36
        STAT, MEAN, VAR, GUESS, HALF, TMP, NOW = 48, 54, 55, 56, 57, 58, 60

        ident = misc[:, IDENT:IDENT + P]
        HC0 = 2 * P + 16

        def head_tab(h, a, n):
            return hc[:, bass.ds(h, 1), a:a + n].rearrange("p a b -> p (a b)")

        def head_col(j):
            return small[:, NOW + j:NOW + j + 1]

        const_in = [sem("const_in_a"), sem("const_in_b")]
        x_in = [sem(f"x_in{t}") for t in range(NT)]
        raw_in = [sem(f"raw_in{i}") for i in range(3)]
        misc_in = sem("misc_in")
        ss_in = [sem(f"sample_state_in{i}") for i in range(2)]
        ss_out = [sem(f"sample_state_out{i}") for i in range(2)]
        st_out, u_out, fixed_out = sem("state_out"), sem("u_out"), sem("fixed_out")
        wo_in = [sem(f"w_out_in{k}") for k in range(3, KT)]
        mi_in = [sem(f"mixed_in{i}") for i in range(2)]
        xr_in = [sem(f"x_again_in{i}") for i in range(2)]
        h2_out = [sem(f"h2_out{i}") for i in range(2)]
        route_in = sem("router_weights_in")
        we_in = [sem(f"expert_weights_in{i}") for i in range(SLOTS)]
        xg_in = [sem(f"xg_in{i}") for i in range(SLOTS)]
        part_out = [sem(f"part_out{i}") for i in range(SLOTS)]
        part_in = [sem(f"part_in{i}") for i in range(3)]
        gfin_in = sem("gfin_in")
        y_out = [sem(f"y_out{i}") for i in range(3)]
        mix_out = [sem(f"mixed_out{i}") for i in range(2)]

        by_pe = {n: sem(n) for n in (
            "xt_mm", "uqk_mm", "g_mm", "v_mm", "kt_mm", "sc_mm", "o_mm", "kv_mm", "skv_mm", "so_mm",
            "ht_mm", "ut_mm", "ct_mm", "w_mm", "t2_mm", "l_mm", "count_mm", "list_mm", "xt2_mm", "h_mm",
            "at_mm", "y_mm")}
        by_act = {n: sem(n) for n in (
            "sq_done", "h_hi", "w_hi", "u_ev", "hist_ev", "ut_ev", "kz_ev", "v_ev", "sig_done",
            "m_hi", "sq2_done", "h2a_ev", "exp_done", "xTa_ev", "sig2_done", "aT_ev", "ya_ev", "sq3_done",
            "z_done")}
        by_dve = {n: sem(n) for n in (
            "zeroed", "rms_guessed", "normed", "now_ready", "h_lo", "w_lo", "qk_ev", "wp_ready", "pool_ready", "scm_done", "qx_done",
            "state_new", "guess_done", "o_used", "on_ready", "pg_ready", "kblk_done", "qm_done", "s_upd",
            "m_lo", "x2_done", "guess2_done", "h2_done", "h2b_ev", "lg_done", "exp_ready", "chosen_done",
            "hot_done", "routed", "xTb_ev", "a_done", "yb_ev", "x3_done", "rstd3_done")}
        by_pool = {n: sem(n) for n in (
            "rms_ready", "sgn_done", "rstd_done", "sum_done", "rstd2_done", "gathered_init", "icol_done", "jcol_done",
            "parts_ready", "y_done")}
        by_sp = {n: sem(n) for n in ("head_stored",)}
        S = {**by_pe, **by_act, **by_dve, **by_pool, **by_sp}
        steps_dve, steps_f, steps_pool = sem("steps_dve"), sem("steps_f"), sem("steps_pool")
        carrier = {n: sem(f"carry_{n}") for n in ("pool", "sp", "dve")}

        def begin(eng, own):
            for s in own.values():
                eng.sem_inc(s, 1)

        def seen(eng, name, n):
            if isinstance(n, int) and n <= 0:
                return
            eng.wait_ge(S[name], n + 1)

        def carried(eng, who):
            eng.sem_inc(carrier[who], 1)

        block = ctx.enter_context(nc.Block())

        def piece(q, h):
            if q < 6:
                j, k = q // 2, 4 * (q % 2)
                col = (0, 512, 1024)[j] + h * P
                return w_in[:, k:k + 4, bass.ds(col, P)], [w[:, j, k:k + 4, :] for w in wuqk], (4, P)
            j, k = (q - 6) // 4, 2 * ((q - 6) % 4)
            col = (1536, 2560, 3584)[j] + h * DV
            return w_in[:, k:k + 2, bass.ds(col, DV)], [w[:, j, k:k + 2, :] for w in wvg], (2, DV)

        def load_piece(eng, q, h, n):
            seen(eng, "w_lo", n - 2)
            src, _, (k, w) = piece(q, h)
            eng.dma_start(raw[q % 3][:, :].rearrange("p (k n) -> p k n", k=k), src).then_inc(raw_in[q % 3], 16)

        def slot_count(h, q):
            return 16 * (6 * h + q // 3 + 1)

        def tiles(eng, step):
            step(0, 0)
            step(1, 1)
            with eng.Fori(1, CH // 2) as i:
                for s in range(2):
                    step(2 * i + s, s)
            step(CH, 0)

        def is_first(t, n):
            return isinstance(t, int) and t < n

        def row_tile(buf, t):
            return buf[:, t, :] if isinstance(t, int) else buf[:, bass.ds(t, 1), :].rearrange("p a n -> p (a n)")

        WOUT0 = 18 * H

        def load_wout(eng, q):
            seen(eng, "w_lo", WOUT0 + q - 2)
            eng.dma_start(raw[q % 3][:, :], w_out[:, q // 2, (q % 2) * 512:(q % 2 + 1) * 512])\
                .then_inc(raw_in[q % 3], 16)

        def load_wout_rest(eng):
            for k in range(3, KT):
                eng.dma_start(wo_raw[k - 3][:, :], w_out[:, k, :]).then_inc(wo_in[k - 3], 16)

        def round_wout_rest(act):
            for k in range(3, KT):
                act.wait_ge(wo_in[k - 3], 16)
                act.activation(wo[k][0][:, :], wo_raw[k - 3][:, :], ACT.Copy).then_inc(S["w_hi"], 1)

        def low_wout_rest(dve, i):
            for k in (3 + i,) if i < 3 else (6, 7):
                seen(dve, "w_hi", WOUT0 + 6 + k - 2)
                dve.tensor_tensor(wo[k][1][:, :], wo_raw[k - 3][:, :], wo[k][0][:, :], ALU.subtract)\
                    .then_inc(S["w_lo"], 1)

        def wout_half(q, which):
            return wo[q // 2][which][:, (q % 2) * 512:(q % 2 + 1) * 512]

        def round_wout(act, q):
            act.wait_ge(raw_in[q % 3], 16 * (WOUT0 // 3 + q // 3 + 1))
            act.activation(wout_half(q, 0), raw[q % 3][:, :], ACT.Copy).then_inc(S["w_hi"], 1)

        def low_wout(dve, q):
            dve.tensor_tensor(wout_half(q, 1), raw[q % 3][:, :], wout_half(q, 0), ALU.subtract)\
                .then_inc(S["w_lo"], 1)

        def expert_weights(sp, e, s):
            def one(w, e):
                return w[0, e] if isinstance(e, int) else w[0, bass.ds(e, 1)].rearrange("a d f -> (a d) f")
            for j, w in enumerate((w1, w3)):
                sp.dma_start(w13[s][:, j, :, :].rearrange("p k f -> p (k f)"),
                             one(w, e).rearrange("(p k) f -> p (k f)", p=P)).then_inc(we_in[s], 16)
            sp.dma_start(w2t[s][:, :, :].rearrange("p i n -> p (i n)"),
                         one(w2, e).rearrange("(p i) n -> p (i n)", p=P)).then_inc(we_in[s], 16)

        GROUPS = NE // SLOTS

        def blocks(eng, step):
            for s in range(SLOTS):
                step(s, s, 0)
            with eng.Fori(1, GROUPS - 1) as g:
                for s in range(SLOTS):
                    step(SLOTS * g + s, s, g)
            for s in range(SLOTS):
                step(NE - SLOTS + s, s, GROUPS - 1)

        def spilled(eng, step):
            many = eng.value_load(spill[0:1, 2 * SPILL:2 * SPILL + 1], min_val=0, max_val=SPILL)
            with eng.If(many > 0):
                with eng.Fori(0, SPILL) as i:
                    live = eng.value_load(spill[0:1, bass.ds(i, 1)], min_val=0, max_val=1)
                    with eng.If(live > 0):
                        step(NE + i, i)
                    eng.nop()
                eng.nop()

        def load_mixed(sp, t, s):
            if not is_first(t, 2):
                seen(sp, "ct_mm", 2 * (t - 1))
                if not isinstance(t, int):
                    carried(sp, "sp")
            sp.wait_ge(mix_out[s], 16 * ((5 - s) * (H - 1) + 1) + (16 * (t // 2) if isinstance(t, int)
                                                                  else 8 * (t - s)))
            if not isinstance(t, int):
                carried(sp, "sp")
            if isinstance(t, int) and t == CH:
                sp.dma_start(mi[s][0:NB, :], mixed_d[SEQ:NTOK, :]).then_inc(mi_in[s], 16)
            else:
                sp.dma_start(mi[s][:, :], mixed_d[bass.ds(t * P, P), :]).then_inc(mi_in[s], 16)

        def load_x(sp, t, s):
            if not is_first(t, 2):
                seen(sp, "x2_done", 2 * (t - 1))
                if not isinstance(t, int):
                    carried(sp, "sp")
            if isinstance(t, int) and t == CH:
                sp.dma_start(xr[s][0:NB, :], x_s).then_inc(xr_in[s], 16)
            else:
                sp.dma_start(xr[s][:, :], x_p[bass.ds(t * P, P), :]).then_inc(xr_in[s], 16)

        def first_loads_c(sp, i):
            if i == 0:
                seen(sp, "v_mm", 9 * H)
                load_wout_rest(sp)
            elif i == 1:
                seen(sp, "qk_ev", 6 * H)
                load_mixed(sp, 0, 0)
                load_x(sp, 0, 0)
                load_mixed(sp, 1, 1)

        def stage_c_sp(sp):
            seen(sp, "sum_done", 9 * H)
            sp.dma_start(gffn_b[:, :], g_ffn[0:1, :].to_broadcast([P, D])).then_inc(route_in, 16)
            sp.dma_start(wr[:, :, 0:4], w_grp[0].rearrange("(k p) g -> p k g", p=P)).then_inc(route_in, 16)
            sp.dma_start(wr[:, :, 4:36], w_exp[0].rearrange("(k p) g e -> p k (g e)", p=P))\
                .then_inc(route_in, 16)
            with sp.Fori(1, CH // 2) as i:
                for s in range(2):
                    load_mixed(sp, 2 * i + s, s)
                    load_x(sp, 2 * i + s - 1, 1 - s)
            load_mixed(sp, CH, 0)
            load_x(sp, CH - 1, 1)
            load_x(sp, CH, 0)

            def weights(b, s, g):
                if is_first(b, 3):
                    seen(sp, "w_mm", NT)
                elif is_first(b, 4):
                    seen(sp, "list_mm", 1)
                else:
                    seen(sp, "y_mm", b - 3)
                    if not isinstance(b, int):
                        carried(sp, "sp")
                expert_weights(sp, b, s)

            blocks(sp, weights)
            seen(sp, "routed", 1)

            def more(b, i):
                seen(sp, "y_mm", b)
                carried(sp, "sp")
                e = sp.value_load(spill[0:1, bass.ds(i + SPILL, 1)], min_val=0, max_val=NE - 1)
                expert_weights(sp, e, 0)

            spilled(sp, more)

            seen(sp, "parts_ready", 1)
            for t in range(NT):
                rows = P if t < CH else NB
                seen(sp, "x3_done", t - 2)
                sp.dma_start(parts[t % 3][0:rows, :, :].rearrange("p j n -> p (j n)"),
                             part_d[2 * t * P:2 * (t * P + rows), :].rearrange("(p j) n -> p (j n)", j=2))\
                    .then_inc(part_in[t % 3], 16)
                if t == 1:
                    sp.dma_start(gfin_b[:, :], g_final.unsqueeze(0).to_broadcast([P, D])).then_inc(gfin_in, 16)
            for t in range(NT):
                rows = P if t < CH else NB
                dst = y_prompt[0, t * P:(t + 1) * P, :] if t < CH else y_sample.rearrange("b o d -> (b o) d")
                seen(sp, "y_done", t + 1)
                sp.dma_start(dst, zt[t % 3][0:rows, :]).then_inc(y_out[t % 3], 16)
            for s in range(3):
                sp.wait_ge(y_out[s], 16 * 3)

        def stage_c_act(act):
            seen(act, "v_mm", 9 * H)
            round_wout_rest(act)

            def high(t, s):
                for b in range(2):
                    seen(act, "ct_mm", 2 * t + b + 1)
                    seen(act, "w_mm", t - 1)
                    act.activation(mT[s][0][:, 4 * b:4 * b + 4, :].rearrange("p k n -> p (k n)"), banks[b][:, :],
                                   ACT.Copy).then_inc(S["m_hi"], 1)

            def h2_out_of_psum(t, s):
                seen(act, "t2_mm", 2 * t + 1)
                seen(act, "l_mm", t - 1)
                act.activation(h2T[s][:, 0:4, :].rearrange("p k n -> p (k n)"), banks[6][:, :], ACT.Copy)\
                    .then_inc(S["h2a_ev"], 1)

            def step(t, s):
                if not (isinstance(t, int) and t == CH):
                    high(t + 1, 1 - s)
                if not is_first(t, 1):
                    h2_out_of_psum(t - 1, 1 - s)
                seen(act, "x2_done", 2 * t + 2)
                seen(act, "sq2_done", t)
                seen(act, "h2_done", t - 1)
                act.activation(junk_c[:, :], row_tile(x2, t), ACT.Square,
                               accum_out=small[:, SS + s:SS + s + 1]).then_inc(S["sq2_done"], 1)

            high(0, 0)
            tiles(act, step)
            h2_out_of_psum(CH, 0)
            seen(act, "exp_ready", 1)
            act.activation(tmp_e[:, 0:NT, 0:4], tmp_e[:, 0:NT, 4:8], ACT.Exp).then_inc(S["exp_done"], 1)
            seen(act, "exp_ready", 2)
            act.activation(vec[:, 6, 0:NT], vec[:, 5, 0:NT], ACT.Exp).then_inc(S["exp_done"], 1)

            def x_out_of_psum(b, s2):
                seen(act, "xt2_mm", 2 * b + 1)
                seen(act, "h_mm", b - 1)
                act.activation(xT[s2][:, 0:4, :].rearrange("p k n -> p (k n)"), banks[0][:, :], ACT.Copy)\
                    .then_inc(S["xTa_ev"], 1)

            def sigmoid(b, s2):
                seen(act, "h_mm", b + 1)
                seen(act, "a_done", b - 1)
                act.activation(sig[s2][:, :], banks[2 + s2][:, 0:FE], ACT.Sigmoid).then_inc(S["sig2_done"], 1)

            def a_out_of_psum(b, s2):
                seen(act, "at_mm", b + 1)
                seen(act, "y_mm", b - 1)
                act.activation(aT[s2][:, :, :].rearrange("p i n -> p (i n)"), banks[4][:, 0:2 * P], ACT.Copy)\
                    .then_inc(S["aT_ev"], 1)

            def y_out_of_psum(b, s2):
                seen(act, "y_mm", b + 1)
                act.activation(yb[s2][:, 0:512], banks[5][:, :], ACT.Copy).then_inc(S["ya_ev"], 1)

            def step_m(b, s, g):
                sigmoid(b, s % 2)
                if not is_first(b, 1):
                    stored_before(act, b - 1, (s - 1) % SLOTS, g if s > 0 else g - 1)
                    y_out_of_psum(b - 1, (s - 1) % 2)
                if not (isinstance(b, int) and b == NE - 1):
                    x_out_of_psum(b + 1, (s + 1) % 2)
                a_out_of_psum(b, s % 2)

            seen(act, "routed", 1)
            x_out_of_psum(0, 0)
            blocks(act, step_m)
            stored_before(act, NE - 1, SLOTS - 1, GROUPS - 1)
            y_out_of_psum(NE - 1, 1)

            def more(b, i):
                x_out_of_psum(b, 0)
                sigmoid(b, 0)
                a_out_of_psum(b, 0)
                y_is_stored(act, i)
                y_out_of_psum(b, 0)

            spilled(act, more)

            seen(act, "parts_ready", 1)
            for t in range(NT):
                seen(act, "x3_done", t + 1)
                seen(act, "sq3_done", t)
                act.activation(junk_f[:, :], x2[:, t, :], ACT.Square, accum_out=small[:, SS + t:SS + t + 1])\
                    .then_inc(S["sq3_done"], 1)
                for u in ready_by(t):
                    seen(act, "rstd3_done", u // 3 + 1)
                    if u >= 3:
                        act.wait_ge(y_out[u % 3], 16 * (u // 3))
                    act.activation(zt[u % 3][:, :], x2[:, u, :], ACT.Identity, scale=small[:, RS + u:RS + u + 1])\
                        .then_inc(S["z_done"], 1)

        def ready_by(t):
            return {2: (), 5: (0, 1, 2), 8: (3, 4, 5, 6, 7, 8)}.get(t, ())

        def stored_before(eng, b, s, g):
            if is_first(b, 2):
                return
            s2, g2 = (s - 2, g) if s >= 2 else (s + 2, g - 1)
            eng.wait_ge(part_out[s2], 16 * (g2 + 1))

        def y_is_stored(eng, i):
            eng.wait_ge(part_out[2], 16 * GROUPS)
            eng.wait_ge(part_out[0], 16 * (GROUPS + i))

        def stage_c_pe(pe, last_samples):
            for n in range(3):
                last_samples(n)
            seen(pe, "sig_done", 9 * H)
            seen(pe, "kz_ev", 9 * H)

            def mixed_over(t, s):
                for b in range(2):
                    if b == 0:
                        pe.wait_ge(mi_in[s], 16 * (t // 2 + 1) if isinstance(t, int) else 8 * (t - s) + 16)
                    seen(pe, "m_lo", 2 * (t - 1) + b + 1)
                    for j in range(4):
                        mm = pe.transpose(banks[b][:, j * P:(j + 1) * P], mi[s][:, (4 * b + j) * P:(4 * b + j + 1) * P],
                                          ident)
                    mm.then_inc(S["ct_mm"], 1)

            def out_product(t, s):
                seen(pe, "m_lo", 2 * t + 2)
                seen(pe, "x2_done", 2 * (t - 1))
                if is_first(t, 1):
                    seen(pe, "w_lo", WOUT0 + 6 + KT - 3)
                for k in range(KT):
                    for xi, wi in ((0, 0), (0, 1), (1, 0)):
                        for n in range(2):
                            mm = pe.matmul(banks[2 + 2 * s + n][:, :], mT[s][xi][:, k, :],
                                           wo[k][wi][:, n * 512:(n + 1) * 512], start=(k == 0 and xi + wi == 0),
                                           stop=(k == KT - 1 and xi == 1))
                mm.then_inc(S["w_mm"], 1)

            def h2_over(t, s):
                seen(pe, "h2_done", t + 1)
                for b in range(2):
                    seen(pe, "lg_done" if b == 0 else "h2b_ev", t)
                    for j in range(4):
                        k = 4 * b + j
                        mm = pe.transpose(banks[6 + b][:, j * P:(j + 1) * P], h2[s][:, k * P:(k + 1) * P], ident)
                    mm.then_inc(S["t2_mm"], 1)

            def router(t, s):
                seen(pe, "h2a_ev", t + 1)
                seen(pe, "h2b_ev", t + 1)
                if is_first(t, 1):
                    pe.wait_ge(route_in, 48)
                for k in range(KT):
                    mm = pe.matmul(banks[6][:, 0:36], h2T[s][:, k, :], wr[:, k, :], start=(k == 0),
                                   stop=(k == KT - 1))
                mm.then_inc(S["l_mm"], 1)

            def step(t, s):
                if not (isinstance(t, int) and t == CH):
                    mixed_over(t + 1, 1 - s)
                if not is_first(t, 2):
                    router(t - 2, s)
                out_product(t, s)
                if not is_first(t, 1):
                    h2_over(t - 1, 1 - s)

            mixed_over(0, 0)
            for n in range(3, 5):
                last_samples(n)
            tiles(pe, step)
            router(CH - 1, 1)
            h2_over(CH, 0)
            router(CH, 0)

            seen(pe, "chosen_done", 1)
            flat = both[:, :, :].rearrange("p t e -> p (t e)")
            pe.matmul(banks[0][:, 0:NT * NE], misc[:, BEFORE:BEFORE + P], flat, start=True, stop=True)
            pe.matmul(banks[1][:, 0:NT * NE], misc[:, ONES:ONES + P], flat, start=True, stop=True)\
                .then_inc(S["count_mm"], 1)
            seen(pe, "hot_done", 1)
            for i in range(2 * NT):
                mm = pe.matmul(banks[2][:, 0:3 * NBLK], slot_hot[:, i, :], planes[:, i, :], start=(i == 0),
                               stop=(i == 2 * NT - 1))
            mm.then_inc(S["list_mm"], 1)

            def x_over(b, s, g):
                pe.wait_ge(xg_in[s], 16 * (g + 1))
                view = xg[s][:, :].rearrange("p (d k) -> p k d", k=KT)
                for n in range(2):
                    seen(pe, "xTa_ev" if n == 0 else "xTb_ev", b)
                    for j in range(4):
                        mm = pe.transpose(banks[n][:, j * P:(j + 1) * P], view[:, 4 * n + j, :], ident)
                    mm.then_inc(S["xt2_mm"], 1)

            def up(b, s, s2, g):
                seen(pe, "xTa_ev", b + 1)
                seen(pe, "xTb_ev", b + 1)
                seen(pe, "a_done", b - 1)
                pe.wait_ge(we_in[s], 48 * (g + 1))
                out = banks[2 + s2][:, :].rearrange("p (j f) -> p j f", j=2)
                for k in range(KT):
                    mm = pe.matmul(out, xT[s2][:, k, :], w13[s][:, :, k, :], start=(k == 0), stop=(k == KT - 1))
                mm.then_inc(S["h_mm"], 1)

            def a_over(b, s2):
                seen(pe, "a_done", b + 1)
                seen(pe, "aT_ev", b)
                view = aa[s2][:, :].rearrange("p (f i) -> p i f", i=2)
                for i in range(2):
                    mm = pe.transpose(banks[4][:, i * P:(i + 1) * P], view[:, i, :], ident)
                mm.then_inc(S["at_mm"], 1)

            def down(b, s, s2):
                seen(pe, "aT_ev", b + 1)
                seen(pe, "ya_ev", b)
                seen(pe, "yb_ev", b)
                for n in range(2):
                    for i in range(2):
                        mm = pe.matmul(banks[5 + n][:, :], aT[s2][:, i, :], w2t[s][:, i, n * 512:(n + 1) * 512],
                                       start=(i == 0), stop=(i == 1))
                mm.then_inc(S["y_mm"], 1)

            def step_m(b, s, g):
                up(b, s, s % 2, g)
                if not is_first(b, 1):
                    down(b - 1, (s - 1) % SLOTS, (s - 1) % 2)
                if not (isinstance(b, int) and b == NE - 1):
                    x_over(b + 1, (s + 1) % SLOTS, g if s < SLOTS - 1 else g + 1)
                a_over(b, s % 2)

            x_over(0, 0, 0)
            blocks(pe, step_m)
            down(NE - 1, SLOTS - 1, 1)
            seen(pe, "routed", 1)

            def more(b, i):
                x_over(b, 0, GROUPS + i)
                up(b, 0, 0, GROUPS + i)
                a_over(b, 0)
                down(b, 0, 0)

            spilled(pe, more)

        def low_mixed(dve, t, s):
            for b in range(2):
                seen(dve, "m_hi", 2 * t + b + 1)
                at = (slice(None), slice(4 * b, 4 * b + 4), slice(None))
                dve.tensor_tensor(mT[s][1][at].rearrange("p k n -> p (k n)"), banks[b][:, :],
                                  mT[s][0][at].rearrange("p k n -> p (k n)"), ALU.subtract)\
                    .then_inc(S["m_lo"], 1)

        def stage_c_dve(dve, done):
            steps = Steps(dve, steps_dve)
            def logits_out(t):
                seen(dve, "l_mm", t + 1)
                dve.tensor_copy(row_tile(logits, t), banks[6][:, 0:36]).then_inc(S["lg_done"], 1)

            def h2_out_of_psum(t, s):
                seen(dve, "t2_mm", 2 * t + 2)
                seen(dve, "l_mm", t - 1)
                dve.tensor_copy(h2T[s][:, 4:8, :].rearrange("p k n -> p (k n)"), banks[7][:, :])\
                    .then_inc(S["h2b_ev"], 1)

            def step(t, s, start, index):
                steps.round_(start, index, 4)
                steps.n = 2 * s
                if not (isinstance(t, int) and t == CH):
                    low_mixed(dve, t + 1, 1 - s)
                if not is_first(t, 2):
                    logits_out(t - 2)
                seen(dve, "w_mm", t + 1)
                dve.wait_ge(xr_in[s], 16 * (t // 2 + 1) if isinstance(t, int) else 8 * (t - s) + 16)
                dst = row_tile(x2, t)
                for n in range(2):
                    half = slice(n * 512, (n + 1) * 512)
                    dve.tensor_tensor(dst[:, half], banks[2 + 2 * s + n][:, :], xr[s][:, half], ALU.add)\
                        .then_inc(S["x2_done"], 1)
                if not is_first(t, 1):
                    h2_out_of_psum(t - 1, 1 - s)
                ms, rs = small[:, MS + s:MS + s + 1], small[:, RS + s:RS + s + 1]
                seen(dve, "sq2_done", t + 1)
                steps.do(dve.tensor_scalar(ms, small[:, SS + s:SS + s + 1], 1.0 / D, EPS, ALU.mult, ALU.add))
                rsqrt_guess(steps, dve, ms, rs, bits[:, 0:1]).then_inc(S["guess2_done"], 1)
                seen(dve, "rstd2_done", t + 1)
                seen(dve, "t2_mm", 2 * (t - 1))
                if not is_first(t, 2):
                    dve.wait_ge(h2_out[s], 16 * (t // 2) if isinstance(t, int) else 8 * (t - s))
                dve.scalar_tensor_tensor(out=h2[s][:, :], in0=dst, scalar=rs, in1=gffn_b[:, :],
                                         op0=ALU.mult, op1=ALU.mult).then_inc(S["h2_done"], 1)

            dve.wait_ge(route_in, 48)
            step(0, 0, done, 0)
            step(1, 1, done, 0)
            with dve.Fori(1, CH // 2) as i:
                for s in range(2):
                    step(2 * i + s, s, done, i)
            step(CH, 0, done, CH // 2)
            logits_out(CH - 1)
            h2_out_of_psum(CH, 0)
            logits_out(CH)

            steps.base, steps.n = done + 4 * (CH // 2) + 2, 0
            seen(dve, "lg_done", NT)
            route(dve, steps)

            start = steps.base + steps.n

            def x_out_of_psum(b, s2):
                seen(dve, "xt2_mm", 2 * b + 2)
                seen(dve, "h_mm", b - 1)
                dve.tensor_copy(xT[s2][:, 4:8, :].rearrange("p k n -> p (k n)"), banks[1][:, :])\
                    .then_inc(S["xTb_ev"], 1)

            def gate(b, s2):
                steps.round_(start, b, 1)
                seen(dve, "sig2_done", b + 1)
                seen(dve, "a_done", b)
                steps.do(dve.tensor_tensor(act1[:, :], banks[2 + s2][:, 0:FE], sig[s2][:, :], ALU.mult))
                seen(dve, "at_mm", b - 1)
                dve.tensor_tensor(aa[s2][:, :], banks[2 + s2][:, FE:2 * FE], act1[:, :], ALU.mult)\
                    .then_inc(S["a_done"], 1)

            def y_out_of_psum(b, s2):
                seen(dve, "y_mm", b + 1)
                seen(dve, "ya_ev", b + 1)
                dve.tensor_copy(yb[s2][:, 512:D], banks[6][:, :]).then_inc(S["yb_ev"], 1)

            def step_m(b, s, g):
                gate(b, s % 2)
                if not is_first(b, 1):
                    y_out_of_psum(b - 1, (s - 1) % 2)
                if not (isinstance(b, int) and b == NE - 1):
                    x_out_of_psum(b + 1, (s + 1) % 2)

            x_out_of_psum(0, 0)
            blocks(dve, step_m)
            y_out_of_psum(NE - 1, 1)

            def more(b, i):
                x_out_of_psum(b, 0)
                gate(b, 0)
                y_out_of_psum(b, 0)

            spilled(dve, more)

            seen(dve, "parts_ready", 1)
            many = Steps(dve, steps_f)

            def add_parts(t):
                dve.wait_ge(part_in[t % 3], 16 * (t // 3 + 1))
                many.do(dve.scalar_tensor_tensor(out=x2[:, t, :], in0=parts[t % 3][:, 0, :], scalar=pair_w[:, t, 0:1],
                                                 in1=x2[:, t, :], op0=ALU.mult, op1=ALU.add))
                dve.scalar_tensor_tensor(out=x2[:, t, :], in0=parts[t % 3][:, 1, :], scalar=pair_w[:, t, 1:2],
                                         in1=x2[:, t, :], op0=ALU.mult, op1=ALU.add).then_inc(S["x3_done"], 1)

            def norms(r):
                seen(dve, "sq3_done", 3 * r + 3)
                a, b = 3 * r, 3 * r + 3
                many.do(dve.tensor_scalar(small[:, MS + a:MS + b], small[:, SS + a:SS + b], 1.0 / D, EPS,
                                          ALU.mult, ALU.add))
                many.do(rsqrt_guess(many, dve, small[:, MS + a:MS + b], small[:, RS + a:RS + b], bits[:, a:b]))
                newton_rsqrt(many, dve, small[:, MS + a:MS + b], small[:, RS + a:RS + b], small[:, HX + a:HX + b],
                             small[:, TX + a:TX + b]).then_inc(S["rstd3_done"], 1)

            for t in range(NT):
                add_parts(t)
                if t in (3, 6):
                    norms(t // 3 - 1)
            norms(2)

        def route(dve, st):
            do = st.do
            rev8 = misc[:, REV:REV + 8].unsqueeze(1).to_broadcast([P, NT, 8])
            rev4 = misc[:, REV + 4:REV + 8].unsqueeze(1).to_broadcast([P, NT, 4])
            live = misc[:, LIVE:LIVE + 2 * NT]
            lg, le4 = logits[:, :, 0:4], logits[:, :, 4:36].rearrange("p t (g e) -> p t g e", g=4)
            top, rank, total, m1, m2, d12, e12, pg = (vec[:, i, 0:NT] for i in range(8))
            pos, q, rem, exp_id, adj, blk = (vec[:, i, :] for i in range(8, 14))
            goh, eq4, d4 = tmp_e[:, 0:NT, 8:12], tmp_e[:, 0:NT, 12:16], tmp_e[:, 0:NT, 4:8]
            le, oh1, oh2 = both[:, :, 0:8], both[:, :, 8:16], both[:, :, 16:24]
            le2, eq8 = both[:, :, 24:32], before_e[:, 0:NT, 0:8]

            def along(v, n):
                return v.unsqueeze(2).to_broadcast([P, v.shape[1], n])

            def pick(values, hot, scratch, best, first, rev, n):
                do(dve.tensor_reduce(best, values, AX, ALU.max))
                do(dve.tensor_tensor(scratch, values, along(best, n), ALU.is_equal))
                do(dve.tensor_tensor(scratch, scratch, rev, ALU.mult))
                do(dve.tensor_reduce(first, scratch, AX, ALU.max))
                do(dve.tensor_tensor(hot, rev, along(first, n), ALU.is_equal))

            pick(lg, goh, eq4, top, rank, rev4, 4)
            do(dve.tensor_tensor(d4, lg, along(top, 4), ALU.subtract))
            dve.sem_inc(S["exp_ready"], 1)
            wide = chosen[:, 0:NT, :].rearrange("p t (g e) -> p t g e", g=4)
            do(dve.tensor_tensor(wide, le4, goh.unsqueeze(3).to_broadcast([P, NT, 4, 8]), ALU.mult))
            do(dve.tensor_reduce(le, wide.rearrange("p t g e -> p t e g"), AX, ALU.add))
            pick(le, oh1, eq8, m1, rank, rev8, 8)
            do(dve.scalar_tensor_tensor(out=le2, in0=oh1, scalar=-3e38, in1=le, op0=ALU.mult, op1=ALU.add))
            pick(le2, oh2, eq8, m2, rank, rev8, 8)
            do(dve.tensor_tensor(d12, m2, m1, ALU.subtract))
            dve.sem_inc(S["exp_ready"], 1)
            do(dve.tensor_tensor(goh, goh, along(live[:, 0:2 * NT:2], 4), ALU.mult))
            for j, hot in enumerate((oh1, oh2)):
                do(dve.tensor_tensor(chosen[:, j:2 * NT:2, :].rearrange("p t (g e) -> p t g e", g=4),
                                     goh.unsqueeze(3).to_broadcast([P, NT, 4, 8]),
                                     hot.unsqueeze(2).to_broadcast([P, NT, 4, 8]), ALU.mult))
            dve.tensor_tensor(both[:, :, :], chosen[:, 0:2 * NT:2, :], chosen[:, 1:2 * NT:2, :], ALU.add)\
                .then_inc(S["chosen_done"], 1)
            seen(dve, "exp_done", 2)
            do(dve.tensor_reduce(total, tmp_e[:, 0:NT, 0:4], AX, ALU.add))
            do(dve.reciprocal(pg, total))
            do(dve.tensor_scalar(total, e12, 1.0, None, ALU.add))
            do(dve.reciprocal(total, total))
            do(dve.tensor_tensor(pair_w[:, :, 0], pg, total, ALU.mult))
            do(dve.tensor_tensor(pair_w[:, :, 1], pair_w[:, :, 0], e12, ALU.mult))
            do(dve.memset(before_e[:, 0, :], 0.0))
            seen(dve, "count_mm", 1)
            counts = banks[1][:, 0:NT * NE].rearrange("p (t e) -> p t e", e=NE)
            for t in range(NT):
                do(dve.tensor_tensor(before_e[:, t + 1, :], before_e[:, t, :], counts[:, t, :], ALU.add))
            tot, ov, ovend, adj_e = before_e[:, NT, :], evec[:, 0, :], evec[:, 1, :], evec[:, 2, :]
            do(dve.tensor_tensor(before_e[:, 0:NT, :], before_e[:, 0:NT, :],
                                 banks[0][:, 0:NT * NE].rearrange("p (t e) -> p t e", e=NE), ALU.add))

            def of_own(out, table):
                do(dve.tensor_tensor(tmp_e[:, :, :], chosen[:, :, :], table, ALU.mult))
                do(dve.tensor_reduce(out, tmp_e[:, :, :], AX, ALU.add))

            for j in range(2):
                do(dve.tensor_tensor(tmp_e[:, j:2 * NT:2, :], chosen[:, j:2 * NT:2, :], before_e[:, 0:NT, :],
                                     ALU.mult))
            do(dve.tensor_reduce(pos, tmp_e[:, :, :], AX, ALU.add))
            thr = misc[:, THR:THR + 8]
            t8 = tmp_e[:, :, 0:8]
            do(dve.tensor_tensor(t8, along(pos, 8), thr.unsqueeze(1).to_broadcast([P, 2 * NT, 8]), ALU.is_ge))
            do(dve.tensor_reduce(q, t8, AX, ALU.add))
            do(dve.scalar_tensor_tensor(out=rem, in0=q, scalar=-128.0, in1=pos, op0=ALU.mult, op1=ALU.add))
            o8 = slot_hot[:, 0, :].rearrange("p (e m) -> p e m", m=4)
            wide8 = slot_hot[:, 0:2, :].rearrange("p a (e m) -> p (a e) m", m=8)
            do(dve.tensor_tensor(wide8, along(tot, 8), thr.unsqueeze(1).to_broadcast([P, NE, 8]), ALU.is_gt))
            do(dve.tensor_reduce(ov, wide8, AX, ALU.add))
            do(dve.tensor_tensor_scan(ovend, misc[:, ONES:ONES + NE], ov, 0.0, ALU.mult, ALU.add))
            iota = misc[:, IOTA:IOTA + P]
            do(dve.tensor_tensor(adj_e, ovend, ov, ALU.subtract))
            do(dve.tensor_tensor(adj_e, adj_e, iota[:, 0:NE], ALU.subtract))
            do(dve.tensor_scalar(adj_e, adj_e, NE - 1.0, None, ALU.add))
            of_own(exp_id, iota[:, 0:NE].unsqueeze(1).to_broadcast([P, 2 * NT, NE]))
            of_own(adj, adj_e.unsqueeze(1).to_broadcast([P, 2 * NT, NE]))
            do(dve.tensor_tensor(adj, adj, q, ALU.add))
            do(dve.tensor_scalar(q, q, 1.0, None, ALU.min))
            do(dve.tensor_tensor(adj, adj, q, ALU.mult))
            do(dve.tensor_tensor(blk, exp_id, adj, ALU.add))
            do(dve.tensor_tensor(slot_hot[:, :, :], iota.unsqueeze(1).to_broadcast([P, 2 * NT, P]), along(rem, P),
                                 ALU.is_equal))
            hot = planes[:, :, 0:NBLK]
            do(dve.tensor_tensor(hot, iota[:, 0:NBLK].unsqueeze(1).to_broadcast([P, 2 * NT, NBLK]),
                                 along(blk, NBLK), ALU.is_equal))
            do(dve.tensor_tensor(hot, hot, along(live, NBLK), ALU.mult))
            do(dve.tensor_tensor(planes[:, :, NBLK:2 * NBLK], hot, along(misc[:, TOKC:TOKC + 2 * NT], NBLK), ALU.mult))
            dve.tensor_tensor(planes[:, :, 2 * NBLK:3 * NBLK], hot, along(misc[:, AID:AID + 2 * NT], NBLK), ALU.mult)\
                .then_inc(S["hot_done"], 1)
            w = tmp_e[:, 0:SPILL, :]
            do(dve.tensor_tensor(w, ovend.unsqueeze(1).to_broadcast([P, SPILL, NE]), along(iota[:, 0:SPILL], NE),
                                 ALU.is_le))
            do(dve.tensor_reduce(evec[:, 3, 0:SPILL], w, AX, ALU.add))
            do(dve.tensor_scalar(spill[:, SPILL:2 * SPILL], evec[:, 3, 0:SPILL], NE - 1.0, None, ALU.min))
            do(dve.tensor_scalar(spill[:, 0:SPILL], iota[:, 0:SPILL], ovend[:, NE - 1:NE], None, ALU.is_lt))
            do(dve.tensor_copy(spill[:, 2 * SPILL:2 * SPILL + 1], ovend[:, NE - 1:NE]))
            seen(dve, "list_mm", 1)
            gap = evec[:, :, :].rearrange("p a e -> p (a e)")[:, 0:NBLK]
            do(dve.tensor_scalar(gap, banks[2][:, 0:NBLK], -4096.0, 4096.0, ALU.mult, ALU.add))
            do(dve.tensor_tensor(idx_tok[:, :], gap, banks[2][:, NBLK:2 * NBLK], ALU.add))
            do(dve.tensor_tensor(idx_pair[:, :], gap, banks[2][:, 2 * NBLK:3 * NBLK], ALU.add))
            dve.sem_inc(S["routed"], 1)

        def stage_c_pool(pool, done):
            steps = Steps(pool, steps_pool, carrier["pool"])

            def step(t, s, start, index):
                steps.round_(start, index, 2 * NEWTON)
                steps.n = s * NEWTON
                seen(pool, "guess2_done", t + 1)
                carried(pool, "pool")
                newton_rsqrt(steps, pool, small[:, MS + s:MS + s + 1], small[:, RS + s:RS + s + 1],
                             small[:, HALF:HALF + 1], small[:, TMP:TMP + 1]).then_inc(S["rstd2_done"], 1)
                seen(pool, "h2_done", t + 1)
                carried(pool, "pool")
                if isinstance(t, int) and t == CH:
                    pool.dma_start(h2_d[SEQ:NTOK, :], h2[s][0:NB, :]).then_inc(h2_out[s], 16)
                else:
                    pool.dma_start(h2_d[bass.ds(t * P, P), :], h2[s][:, :]).then_inc(h2_out[s], 16)

            step(0, 0, done, 0)
            step(1, 1, done, 0)
            with pool.Fori(1, CH // 2) as i:
                for s in range(2):
                    step(2 * i + s, s, done, i)
            step(CH, 0, done, CH // 2)
            pool.wait_ge(h2_out[0], 16 * 5)
            pool.wait_ge(h2_out[1], 16 * 4)
            seen(pool, "routed", 1)
            for s in range(SLOTS):
                pool.memset(xg[s][:, :], 0.0).then_inc(S["gathered_init"], 1)
            seen(pool, "gathered_init", SLOTS)

            def gather(b, s, g, after=None):
                if not is_first(b, SLOTS):
                    pool.wait_ge(xg_in[s], 16 * g)
                    carried(pool, "pool")
                    seen(pool, "xt2_mm", after if after is not None else 2 * (b - 3))
                    carried(pool, "pool")
                pool.tensor_copy(icol[s][:, :], idx_tok[:, bass.ds(b, 1)]).then_inc(S["icol_done"], 1)
                seen(pool, "icol_done", b + 1)
                carried(pool, "pool")
                pool.indirect_dma_start(
                    out=xg[s][:, :], out_offset=None, in_=h2_d,
                    in_offset=bass.IndirectOffsetOnAxis(ap=icol[s][:, :], axis=0),
                    bounds_check=NTOK - 1, oob_is_err=False).then_inc(xg_in[s], 16)

            def scatter(b, s, s2, g):
                if not is_first(b, SLOTS):
                    pool.wait_ge(part_out[s], 16 * g)
                    carried(pool, "pool")
                pool.tensor_copy(jcol[s][:, :], idx_pair[:, bass.ds(b, 1)]).then_inc(S["jcol_done"], 1)
                for name in ("jcol_done", "ya_ev", "yb_ev"):
                    seen(pool, name, b + 1)
                    carried(pool, "pool")
                pool.indirect_dma_start(
                    out=part_d, out_offset=bass.IndirectOffsetOnAxis(ap=jcol[s][:, :], axis=0),
                    in_=yb[s2][:, :], in_offset=None,
                    bounds_check=2 * NTOK - 1, oob_is_err=False).then_inc(part_out[s], 16)

            gather(0, 0, 0)
            gather(1, 1, 0)

            def step_m(b, s, g):
                if not (isinstance(b, int) and b >= NE - 2):
                    gather(b + 2, (s + 2) % SLOTS, g if s < 2 else g + 1)
                scatter(b, s, s % 2, g)

            blocks(pool, step_m)
            for s in range(SLOTS):
                pool.wait_ge(part_out[s], 16 * GROUPS)

            def more(b, i):
                gather(b, 0, GROUPS + i, after=2 * b)
                scatter(b, 0, 0, GROUPS + i)
                pool.wait_ge(part_out[0], 16 * (GROUPS + i + 1))
                carried(pool, "pool")

            spilled(pool, more)
            pool.sem_inc(S["parts_ready"], 1)

            pool.wait_ge(gfin_in, 16)
            for t in range(NT):
                seen(pool, "z_done", t + 1)
                pool.tensor_tensor(zt[t % 3][:, :], zt[t % 3][:, :], gfin_b[:, :], ALU.mult)\
                    .then_inc(S["y_done"], 1)

        @block.sync
        def _(sp):
            begin(sp, by_sp)
            for t in range(NT):
                rows = P if t < CH else NB
                src = x_p[t * P:(t + 1) * P, :] if t < CH else x_s
                sp.dma_start(xall[0:rows, t, :], src).then_inc(x_in[t], 16)
                if t == 2:
                    sp.dma_start(gmix_b[:, :], g_mix[0:1, :].to_broadcast([P, D])).then_inc(const_in[0], 16)
                    sp.dma_start(misc[:, :], c_misc).then_inc(const_in[0], 16)
                    for q in range(3):
                        load_piece(sp, q, 0, q)
            for q in range(3, 6):
                load_piece(sp, q, 0, q)
                if q == 5:
                    sp.dma_start(cs[:, :, :], c_cs).then_inc(const_in[1], 16)
                    sp.dma_start(hc[:, :, :], c_hc).then_inc(const_in[1], 16)
                    sp.dma_start(gn_b[:, :], ret_gn[0:1, :].to_broadcast([P, D])).then_inc(const_in[1], 16)
            sp.dma_start(pool_s[0, :, 0:HIST - 1, :], state_pool[0, :, 1:HIST, :]).then_inc(fixed_out, 16)

            def states(d, h, g):
                return d[0, 2 * g:2 * g + 2, bass.ds(h, 1)].rearrange("b a d v -> d (b a) v")

            def store_states(h, g):
                seen(sp, "s_upd", 4 * h + g + 1)
                carried(sp, "sp")
                sp.dma_start(states(ret_s, h, g), sst[g % 2][:, :, :]).then_inc(ss_out[g % 2], 16)

            def load_states(h, g):
                if g >= 2:
                    seen(sp, "so_mm", 4 * h + g - 1)
                    carried(sp, "sp")
                    sp.wait_ge(ss_out[g % 2], 32 * h + 16)
                    carried(sp, "sp")
                sp.dma_start(sst[g % 2][:, :, :], states(state_ret, h, g)).then_inc(ss_in[g % 2], 16)

            def tail(h, between):
                between(0)
                store_states(h, 0)
                between(1)
                store_states(h, 1)
                load_states(h, 2)
                between(2)
                load_states(h, 3)
                between(3)
                store_states(h, 2)
                store_states(h, 3)
                for s, v in ((ss_out[0], 32), (ss_out[1], 32), (st_out, 16), (u_out, 32)):
                    sp.wait_ge(s, v * h + v)
                    carried(sp, "sp")
                sp.sem_inc(S["head_stored"], 1)

            def head(h, first, last):
                if not first:
                    def pieces(i):
                        for q in range(6 + 3 * i, 9 + 3 * i):
                            load_piece(sp, q, h, 18 * h + q)
                    tail(h - 1, pieces)
                    seen(sp, "o_mm", 8 * h)
                    carried(sp, "sp")
                sp.dma_start(hist[0:NB * HIST, :], state_pool[0].rearrange("b r c -> (b r) c")
                             [:, bass.ds(h * P, P)]).then_inc(misc_in, 16)
                if not first:
                    seen(sp, "wp_ready", h)
                    carried(sp, "sp")
                sp.dma_start(wp_raw[:, :], w_pool[0, bass.ds(h, 1)].rearrange("a c d -> (a c) d"))\
                    .then_inc(misc_in, 16)
                sp.dma_start(ps_b[:, :], pool_scale[0:1, bass.ds(h * DV, DV)].to_broadcast([P, DV]))\
                    .then_inc(misc_in, 16)
                if first:
                    for q in range(6, 18):
                        load_piece(sp, q, h, 18 * h + q)
                if not last:
                    for q in range(6):
                        load_piece(sp, q, h + 1, 18 * (h + 1) + q)
                else:
                    for q in range(6):
                        load_wout(sp, q)
                if not first:
                    seen(sp, "so_mm", 4 * h)
                    carried(sp, "sp")
                for g in range(2):
                    load_states(h, g)
                seen(sp, "ut_ev", h + 1)
                carried(sp, "sp")
                sp.dma_start(pool_p[0, 0, :, bass.ds(h * P, P)], uout[P - HIST:P, 0, :]).then_inc(u_out, 16)
                sp.dma_start(pool_s[0, :, HIST - 1:HIST, bass.ds(h * P, P)].rearrange("b a c -> (b a) c"),
                             uout[15:P:16, 1, :]).then_inc(u_out, 16)
                seen(sp, "state_new", 8 * h + 8)
                carried(sp, "sp")
                sp.dma_start(ret_p[0, 0, bass.ds(h, 1)].rearrange("a d v -> (a d) v"), state[:, :])\
                    .then_inc(st_out, 16)

            head(0, True, False)
            with sp.Fori(1, H - 1) as h:
                head(h, False, False)
            head(H - 1, False, True)
            tail(H - 1, lambda i: first_loads_c(sp, i))
            sp.wait_ge(fixed_out, 16)
            stage_c_sp(sp)

        def round_piece(act, q, h, n):
            act.wait_ge(raw_in[q % 3], slot_count(h, q))
            _, (hi, _lo), (k, w) = piece(q, 0)
            act.activation(hi, raw[q % 3][:, :].rearrange("p (k n) -> p k n", k=k), ACT.Copy)\
                .then_inc(S["w_hi"], 1)

        @block.scalar
        def _(act):
            begin(act, by_act)
            seen(act, "zeroed", 1)

            def square(t):
                rows = P if t < CH else NB
                act.wait_ge(x_in[t], 16)
                seen(act, "sq_done", t)
                act.activation(junk_a[0:rows, :], xall[0:rows, t, :], ACT.Square,
                               accum_out=small[0:rows, SS + t:SS + t + 1]).then_inc(S["sq_done"], 1)

            def high_tile(t):
                rows = P if t < CH else NB
                for b in range(2):
                    seen(act, "xt_mm", 2 * t + b + 1)
                    bank = banks[4 + 2 * (t % 2) + b][:, :].rearrange("p (k n) -> p k n", k=4)[:, :, 0:rows]
                    act.activation(hT[0][:, 4 * b:4 * b + 4, t * P:t * P + rows], bank, ACT.Copy)\
                        .then_inc(S["h_hi"], 1)

            for t in range(3):
                square(t)
            for q in range(3):
                round_piece(act, q, 0, q)
            for t in range(3):
                high_tile(t)
                square(3 + t)
            for t in range(6, NT):
                square(t)
            for t in range(3, NT):
                high_tile(t)
                if t < 6:
                    round_piece(act, t, 0, t)

            def head(h, first, last):
                seen(act, "v_mm", 9 * h)
                for n in range(3):
                    for q in range(6 + 3 * n, 9 + 3 * n) if not first else range(6, 9) if n == 2 else ():
                        round_piece(act, q, h, None)
                    seen(act, "uqk_mm", 9 * h + n + 1)
                    if n == 0:
                        seen(act, "pool_ready", h)
                        seen(act, "ut_mm", h)
                    bank = banks[n % 2]
                    if n < 2:
                        act.activation(line[0][:, HIST + n * TC:HIST + (n + 1) * TC], bank[:, 0:TC], ACT.Copy)\
                            .then_inc(S["u_ev"], 1)
                    else:
                        act.activation(line[0][:, HIST + 2 * TC:HIST + SEQ], bank[:, 0:TC - NB], ACT.Copy)
                        act.activation(line[0][:, HIST + SEQ + HIST:SPAN:16], bank[:, TC - NB:TC], ACT.Copy)\
                            .then_inc(S["u_ev"], 1)
                for q in range(9 if first else 15, 18):
                    round_piece(act, q, h, None)
                seen(act, "ht_mm", h + 1)
                tail = line[0][:, HIST + SEQ:SPAN].rearrange("p (b s) -> p b s", s=16)
                act.activation(tail[:, :, 0:HIST], banks[4][:, 0:NB * HIST].rearrange("p (b s) -> p b s", b=NB),
                               ACT.Copy).then_inc(S["hist_ev"], 1)
                seen(act, "ut_mm", h + 1)
                seen(act, "head_stored", h)
                act.activation(uout[:, :, :], banks[5][:, 0:2 * P].rearrange("p (a n) -> p a n", a=2), ACT.Copy)\
                    .then_inc(S["ut_ev"], 1)
                seen(act, "now_ready", h + 1)
                for c in range(NT):
                    lo = 0 if c < CH else Q3
                    seen(act, "kt_mm", 9 * h + c + 1)
                    if c == 0:
                        seen(act, "kblk_done", h)
                    else:
                        seen(act, "kv_mm", 8 * h + c - 1)
                    act.activation(kz[c % 2][lo:P, :], banks[4][lo:P, 0:P], ACT.Copy if c == CH else ACT.Identity,
                                   scale=P ** -0.5 if c == CH else head_col(0)).then_inc(S["kz_ev"], 1)
                    if 1 <= c <= 6:
                        if c == 1:
                            seen(act, "uqk_mm", 9 * h + 9)
                        if not last:
                            round_piece(act, c - 1, h + 1, None)
                        else:
                            round_wout(act, c - 1)
                    seen(act, "v_mm", 9 * h + c + 1)
                    if c < 2:
                        seen(act, "so_mm", 4 * h)
                    else:
                        seen(act, "kv_mm", 8 * h + c - 1)
                    act.activation(vb[c % 2][:, :], banks[2 + c % 2][:, 0:DV], ACT.Copy).then_inc(S["v_ev"], 1)
                    seen(act, "on_ready", 9 * h + c - 1)
                    act.activation(sg[c % 2][:, :], banks[(9 + c) % 2][:, :], ACT.Sigmoid)\
                        .then_inc(S["sig_done"], 1)

            head(0, True, False)
            with act.Fori(1, H - 1) as h:
                head(h, False, False)
            head(H - 1, False, True)
            stage_c_act(act)

        def three(pe, out, lhs, rhs, first, last):
            pe.matmul(out, lhs[0], rhs[0], start=first, stop=False)
            pe.matmul(out, lhs[0], rhs[1], start=False, stop=False)
            return pe.matmul(out, lhs[1], rhs[0], start=False, stop=last)

        @block.tensor
        def _(pe):
            begin(pe, by_pe)
            pe.wait_ge(const_in[0], 32)

            def h_over(t):
                rows = P if t < CH else NB
                seen(pe, "normed", t + 1)
                for b in range(2):
                    seen(pe, "h_lo", 2 * (t - 2) + b + 1)
                    for j in range(4):
                        k = 4 * b + j
                        mm = pe.transpose(banks[4 + 2 * (t % 2) + b][:, j * P:j * P + rows],
                                          xall[0:rows, t, k * P:(k + 1) * P], ident[0:rows, 0:rows])
                    mm.then_inc(S["xt_mm"], 1)

            def attend_samples(h, n):
                def grow(g):
                    seen(pe, "s_upd", 4 * h + g - 1)
                    for i in range(2):
                        mm = pe.matmul(banks[2 + g % 2][:, i * DV:(i + 1) * DV], kblk[Q3:P, 2 * g + i, :],
                                       vb[0][Q3:P, :], start=True, stop=True)
                    mm.then_inc(S["skv_mm"], 1)

                def read(g):
                    seen(pe, "s_upd", 4 * h + g + 1)
                    for i in range(2):
                        b = 2 * g + i
                        mm = pe.matmul(banks[6][Q3:P, 0:DV], qm[:, b, :], sst[g % 2][:, i, :],
                                       start=(b == 0), stop=(b == NB - 1))
                    mm.then_inc(S["so_mm"], 1)

                if n == 0:
                    seen(pe, "kblk_done", h + 1)
                    seen(pe, "v_ev", 9 * h + 9)
                    seen(pe, "qm_done", h + 1)
                    grow(0)
                    grow(1)
                elif n <= 4:
                    if n == 1:
                        seen(pe, "o_used", 9 * h + 8)
                        pe.matmul(banks[6][Q3:P, DV:2 * DV], ps32[:, :], wp[:, :], start=True, stop=True)
                    read(n - 1)
                    if n <= 2:
                        grow(n + 1)

            def head(h, first):
                for n in range(9):
                    j, tc = n // 3, n % 3
                    if first and n < 3:
                        for t in range(3 * n, 3 * n + 3):
                            h_over(t)
                        seen(pe, "h_lo", 6 * (n + 1))
                    elif not first:
                        attend_samples(h - 1, n)
                    if n < 2:
                        seen(pe, "sig_done", 9 * h)
                    elif n < 5:
                        seen(pe, "u_ev", 3 * h + n - 1)
                    else:
                        seen(pe, "qk_ev", 6 * h + n - 4)
                    if tc == 0:
                        seen(pe, "w_lo", 18 * h + 2 * (j + 1))
                    out = banks[n % 2][:, 0:TC]
                    for k in range(KT):
                        mm = three(pe, out, [w[:, j, k, :] for w in wuqk],
                                   [x[:, k, tc * TC:(tc + 1) * TC] for x in hT], k == 0, k == KT - 1)
                    mm.then_inc(S["uqk_mm"], 1)
                    if n == 5:
                        pe.wait_ge(misc_in, 48 * h + 48)
                        seen(pe, "kz_ev", 9 * h)
                        pe.transpose(banks[4][:, 0:NB * HIST], hist[0:NB * HIST, :],
                                     ident[0:NB * HIST, 0:NB * HIST]).then_inc(S["ht_mm"], 1)
                seen(pe, "hist_ev", h + 1)
                seen(pe, "u_ev", 3 * h + 3)
                seen(pe, "scm_done", 8 * h)
                pe.transpose(banks[5][:, 0:P], line[0][:, HIST + SEQ - P:HIST + SEQ], ident)
                pe.transpose(banks[5][:, P:2 * P], line[0][:, HIST + SEQ:SPAN], ident).then_inc(S["ut_mm"], 1)

                def before(c):
                    seen(pe, "kz_ev", 9 * h + c)
                    at = c * P if c < CH else LAST
                    pe.transpose(banks[4][:, 0:P], kT[:, at:at + P], ident).then_inc(S["kt_mm"], 1)
                    if c == CH:
                        return
                    if c == 0:
                        seen(pe, "ut_ev", h + 1)
                        seen(pe, "qk_ev", 6 * h + 6)
                    seen(pe, "scm_done", 8 * h + c)
                    pe.matmul(banks[5][:, 0:P], kT[:, at:at + P], qT[:, at:at + P], start=True, stop=True)\
                        .then_inc(S["sc_mm"], 1)

                def project(c):
                    if c == 0:
                        seen(pe, "w_lo", 18 * h + 18)
                    if c >= 2:
                        seen(pe, "sig_done", 9 * h + c - 1)
                        seen(pe, "v_ev", 9 * h + c - 1)
                    else:
                        seen(pe, "s_upd", 4 * h)
                        seen(pe, "qk_ev", 6 * h + 5 + c)
                    at = c * P if c < CH else LAST
                    gates, v = banks[(9 + c) % 2], banks[2 + c % 2]
                    gates = gates[:, :].rearrange("p (a n) -> p a n", a=2)
                    for k in range(KT):
                        x = [t[:, k, at:at + P] for t in hT]
                        for xi, wi in ((0, 0), (0, 1), (1, 0)):
                            first, last = k == 0 and xi + wi == 0, k == KT - 1 and xi == 1
                            g = pe.matmul(gates, x[xi], wvg[wi][:, 1:3, k, :], start=first, stop=last)
                            m = pe.matmul(v[:, 0:DV], x[xi], wvg[wi][:, 0, k, :], start=first, stop=last)
                    g.then_inc(S["g_mm"], 1)
                    m.then_inc(S["v_mm"], 1)

                def attend(c):
                    s = c % 2
                    seen(pe, "o_used", 9 * h + c)
                    seen(pe, "pool_ready", h + 1)
                    pe.matmul(banks[6][:, DV:2 * DV], line[1][:, HIST + c * P:HIST + (c + 1) * P], wp[:, :],
                              start=True, stop=True)
                    seen(pe, "scm_done", 8 * h + c + 1)
                    seen(pe, "v_ev", 9 * h + c + 1)
                    o = pe.matmul(banks[6][:, 0:DV], scm[s][:, :], vb[s][:, :], start=True, stop=(c == 0))
                    if c > 0:
                        seen(pe, "qx_done", 7 * h + c)
                        seen(pe, "state_new", 8 * h + c)
                        o = pe.matmul(banks[6][:, 0:DV], qx[s][:, :], state[:, :], start=False, stop=True)
                    o.then_inc(S["o_mm"], 1)
                    seen(pe, "kz_ev", 9 * h + c + 1)
                    seen(pe, "state_new", 8 * h + c)
                    pe.matmul(banks[7][:, 0:DV], kz[s][:, :], vb[s][:, :], start=True, stop=True)\
                        .then_inc(S["kv_mm"], 1)

                for c in range(NT):
                    if c == 0:
                        project(0)
                    before(c)
                    if c > 0:
                        project(c)
                    if c > 0:
                        attend(c - 1)

            head(0, True)
            with pe.Fori(1, H) as h:
                head(h, False)
            stage_c_pe(pe, lambda n: attend_samples(H - 1, n))

        def low_piece(dve, q):
            _, (hi, lo), (k, w) = piece(q, 0)
            dve.tensor_tensor(lo, raw[q % 3][:, :].rearrange("p (k n) -> p k n", k=k), hi, ALU.subtract)\
                .then_inc(S["w_lo"], 1)

        @block.vector
        def _(dve):
            begin(dve, by_dve)
            steps = Steps(dve, steps_dve)
            steps.do(dve.memset(line[0][:, 0:HIST], 0.0))
            steps.do(dve.memset(ps32[:, :], 0.0))
            steps.do(dve.memset(small[:, :], 1.0))
            dve.sem_inc(S["zeroed"], 1)

            def rms_guess(a, b):
                seen(dve, "sq_done", b)
                ms, rs = small[:, MS + a:MS + b], small[:, RS + a:RS + b]
                steps.do(dve.tensor_scalar(ms, small[:, SS + a:SS + b], 1.0 / D, EPS, ALU.mult, ALU.add))
                return ms, rs, rsqrt_guess(steps, dve, ms, rs, bits[:, a:b])

            def rms(a, b):
                ms, rs, last = rms_guess(a, b)
                steps.do(last)
                steps.do(newton_rsqrt(steps, dve, ms, rs, small[:, HX + a:HX + b], small[:, TX + a:TX + b]))

            def normalise(t):
                rows = P if t < CH else NB
                dve.scalar_tensor_tensor(out=xall[0:rows, t, :], in0=xall[0:rows, t, :],
                                         scalar=small[0:rows, RS + t:RS + t + 1], in1=gmix_b[0:rows, :],
                                         op0=ALU.mult, op1=ALU.mult).then_inc(S["normed"], 1)

            def low_tile(t):
                rows = P if t < CH else NB
                for b in range(2):
                    seen(dve, "h_hi", 2 * t + b + 1)
                    at = (slice(None), slice(4 * b, 4 * b + 4), slice(t * P, t * P + rows))
                    bank = banks[4 + 2 * (t % 2) + b][:, :].rearrange("p (k n) -> p k n", k=4)[:, :, 0:rows]
                    dve.tensor_tensor(hT[1][at], bank, hT[0][at], ALU.subtract).then_inc(S["h_lo"], 1)

            rms(0, 3)
            dve.wait_ge(const_in[0], 32)
            for t in range(3):
                normalise(t)
            for q in range(3):
                seen(dve, "w_hi", q + 1)
                low_piece(dve, q)
            for t in range(3):
                low_tile(t)
            rms(3, 6)
            for t in range(3, 6):
                normalise(t)
            rms_guess(6, NT)[2].then_inc(S["rms_guessed"], 1)
            for t in range(3, 6):
                low_tile(t)
            seen(dve, "rms_ready", 1)
            for t in range(6, NT):
                normalise(t)
            for t in range(6, NT):
                seen(dve, "w_hi", t - 2)
                low_piece(dve, t - 3)
                low_tile(t)
            dve.wait_ge(const_in[1], 48)
            before_heads = steps.n
            per_head, per_tail = 48, 4

            def finish(h, c):
                r = slice(0 if c < CH else Q3, P)
                s = c % 2
                if c < CH:
                    seen(dve, "o_mm", 8 * h + c + 1)
                else:
                    seen(dve, "so_mm", 4 * h + 4)
                seen(dve, "sig_done", 9 * h + c + 1)
                seen(dve, "sum_done", 9 * h + c)
                o = banks[6][r, 0:DV]
                dve.tensor_tensor(pgate[r, :], banks[6][r, DV:2 * DV], sg[s][r, 0:DV], ALU.mult)\
                    .then_inc(S["pg_ready"], 1)
                steps.do(dve.bn_stats(small[r, STAT:STAT + 6], o))
                carried(dve, "dve")
                steps.do(dve.bn_aggr(small[r, MEAN:MEAN + 2], small[r, STAT:STAT + 6]))
                steps.do(dve.tensor_scalar(small[r, VAR:VAR + 1], small[r, VAR:VAR + 1], EPS, None, ALU.add))
                rsqrt_guess(steps, dve, small[r, VAR:VAR + 1], small[r, GUESS:GUESS + 1], bits[r, 9:10])\
                    .then_inc(S["guess_done"], 1)

            def finish_rest(h, c):
                r = slice(0 if c < CH else Q3, P)
                s = c % 2
                o = banks[6][r, 0:DV]
                seen(dve, "rstd_done", 9 * h + c + 1)
                dve.tensor_scalar(onorm[r, :], o, small[r, MEAN:MEAN + 1], small[r, GUESS:GUESS + 1],
                                  ALU.subtract, ALU.mult).then_inc(S["o_used"], 1)
                seen(dve, "o_used", 9 * h + c + 1)
                seen(dve, "sgn_done", 9 * h + c + 1)
                dve.tensor_tensor(onorm[r, :], onorm[r, :], sgn[s][r], ALU.mult).then_inc(S["on_ready"], 1)

            def tail(h, between):
                n = steps.n
                for g in range(4):
                    seen(dve, "skv_mm", 4 * h + g + 1)
                    dve.wait_ge(ss_in[g % 2], 32 * h + 16 * (g // 2) + 16)
                    dve.scalar_tensor_tensor(
                        out=sst[g % 2][:, :, :], in0=sst[g % 2][:, :, :], scalar=head_col(2),
                        in1=banks[2 + g % 2][:, :].rearrange("p (a n) -> p a n", a=2), op0=ALU.mult, op1=ALU.add)\
                        .then_inc(S["s_upd"], 1)
                    between(g)
                finish(h, CH)
                assert steps.n - n == per_tail, steps.n - n

            def head(h, first, last):
                steps.round_(before_heads - per_tail, h, per_head)
                if first:
                    steps.n = per_tail
                else:
                    def lows(g):
                        for q in range(6 + 3 * g, 9 + 3 * g):
                            seen(dve, "w_hi", 18 * h + q + 1)
                            low_piece(dve, q)
                    tail(h - 1, lows)
                seen(dve, "kz_ev", 9 * h)
                seen(dve, "s_upd", 4 * h)
                dve.tensor_copy(small[:, NOW:NOW + 8], head_tab(h, HC0, 8)).then_inc(S["now_ready"], 1)
                for n in range(3, 9):
                    seen(dve, "uqk_mm", 9 * h + n + 1)
                    seen(dve, "qk_ev", 6 * h + n - 3)
                    bank, dst = banks[n % 2], (qT, kT)[(n - 3) // 3]
                    at = slice((n % 3) * TC, (n % 3 + 1) * TC)
                    dve.tensor_tensor(dst[:, at], bank[:, 0:TC], cs[:, 0, at], ALU.mult)
                    dve.tensor_tensor(rot[0:64, :], bank[64:P, 0:TC], cs[64:P, 1, at], ALU.mult)
                    steps.do(dve.tensor_tensor(rot[64:P, :], bank[0:64, 0:TC], cs[0:64, 1, at], ALU.mult))
                    dve.tensor_tensor(dst[:, at], dst[:, at], rot[:, :], ALU.add).then_inc(S["qk_ev"], 1)
                    if first:
                        for q in range(2 * n, 2 * n + 2):
                            seen(dve, "w_hi", q + 1)
                            low_piece(dve, q)
                    elif n == 3:
                        finish_rest(h - 1, CH)
                dve.wait_ge(misc_in, 48 * h + 48)
                dve.tensor_tensor(wp[:, :], wp_raw[:, :], ps_b[:, :], ALU.mult).then_inc(S["wp_ready"], 1)

                def scores(c):
                    seen(dve, "sc_mm", 8 * h + c + 1)
                    if c > 1:
                        seen(dve, "o_mm", 8 * h + c - 1)
                    dve.tensor_tensor(scm[c % 2][:, :], banks[5][:, 0:P], head_tab(h, 0, P), ALU.mult)\
                        .then_inc(S["scm_done"], 1)
                    if c > 0:
                        dve.tensor_tensor(qx[c % 2][:, :], qT[:, c * P:(c + 1) * P], head_tab(h, P, P), ALU.mult)\
                            .then_inc(S["qx_done"], 1)

                def pool_means():
                    seen(dve, "u_ev", 3 * h + 3)
                    seen(dve, "hist_ev", h + 1)
                    u, a, b = line[0], line[1], line[2]
                    steps.do(dve.tensor_tensor(a[:, 1:SPAN], u[:, 1:SPAN], u[:, 0:SPAN - 1], ALU.add))
                    for level, (src, dst, lo, gap) in enumerate(((a, b, 3, 2), (b, a, 7, 4), (a, b, 15, 8))):
                        steps.do(dve.scalar_tensor_tensor(
                            out=dst[:, lo:SPAN], in0=src[:, lo - gap:SPAN - gap], scalar=head_col(4 + level),
                            in1=src[:, lo:SPAN], op0=ALU.mult, op1=ALU.add))
                    steps.do(dve.tensor_tensor(b[:, HIST:HIST + 16], b[:, HIST:HIST + 16],
                                               head_tab(h, 2 * P, 16), ALU.mult))
                    steps.do(dve.scalar_tensor_tensor(
                        out=a[:, HIST:SPAN], in0=b[:, HIST:SPAN], scalar=head_col(3), in1=u[:, HIST:SPAN],
                        op0=ALU.mult, op1=ALU.subtract))
                    dve.tensor_copy(ps32[:, 24:32], a[:, HIST + SEQ + HIST:SPAN:16]).then_inc(S["pool_ready"], 1)

                def grow_state(c):
                    seen(dve, "kv_mm", 8 * h + c + 1)
                    if c == 0:
                        seen(dve, "head_stored", h)
                        ins = dve.tensor_copy(state[:, :], banks[7][:, 0:DV])
                    else:
                        seen(dve, "state_new", 8 * h + c)
                        ins = dve.scalar_tensor_tensor(out=state[:, :], in0=state[:, :], scalar=head_col(1),
                                                       in1=banks[7][:, 0:DV], op0=ALU.mult, op1=ALU.add)
                    ins.then_inc(S["state_new"], 1)

                for c in range(NT):
                    if c == 0:
                        pool_means()
                    if c < CH:
                        scores(c)
                    if 1 <= c <= 6:
                        seen(dve, "w_hi", 18 * (h + 1) + c)
                        if not last:
                            low_piece(dve, c - 1)
                        else:
                            low_wout(dve, c - 1)
                    if c == CH:
                        seen(dve, "kz_ev", 9 * h + 9)
                        dve.tensor_tensor(kblk[Q3:P, :, :], kz[0][Q3:P, :].unsqueeze(1).to_broadcast([P - Q3, NB, P]),
                                          misc[Q3:P, KMASK:KMASK + NB].unsqueeze(2).to_broadcast([P - Q3, NB, P]),
                                          ALU.mult).then_inc(S["kblk_done"], 1)
                        dve.tensor_tensor(qm[:, :, :], qT[:, SEQ:NTOK].unsqueeze(2).to_broadcast([P, NB, 32]),
                                          misc[:, QMASK:QMASK + NB * 32].rearrange("p (b j) -> p b j", b=NB),
                                          ALU.mult).then_inc(S["qm_done"], 1)
                    if c > 0:
                        grow_state(c - 1)
                        finish(h, c - 1)
                        finish_rest(h, c - 1)
                assert steps.n == per_head, steps.n

            head(0, True, False)
            with dve.Fori(1, H - 1) as h:
                head(h, False, False)
            head(H - 1, False, True)
            steps.round_(before_heads - per_tail, H, per_head)

            def lows(g):
                low_wout_rest(dve, g)
                if g == 3:
                    low_mixed(dve, 0, 0)
            tail(H - 1, lows)
            finish_rest(H - 1, CH)
            stage_c_dve(dve, before_heads + H * per_head)

        @block.gpsimd
        def _(pool):
            begin(pool, by_pool)
            steps = Steps(pool, steps_pool, carrier["pool"])
            seen(pool, "rms_guessed", 1)
            newton_rsqrt(steps, pool, *(small[:, a + 6:a + NT] for a in (MS, RS, HX, TX)))\
                .then_inc(S["rms_ready"], 1)
            pool.wait_ge(const_in[1], 48)
            per_head = 9 * NEWTON

            def head(h):
                steps.round_(NEWTON, h, per_head)
                for c in range(NT + 1):
                    if c < NT:
                        s = c % 2
                        seen(pool, "sig_done", 9 * h + c + 1)
                        carried(pool, "pool")
                        pool.tensor_tensor(sgn[s], sgn[s], gn_b[:, bass.ds(h * DV, DV)],
                                           ALU.mult).then_inc(S["sgn_done"], 1)
                    if c == 0:
                        continue
                    c1 = c - 1
                    s = c1 % 2
                    seen(pool, "guess_done", 9 * h + c1 + 1)
                    carried(pool, "pool")
                    newton_rsqrt(steps, pool, small[:, VAR:VAR + 1], small[:, GUESS:GUESS + 1],
                                 small[:, HALF:HALF + 1], small[:, TMP:TMP + 1]).then_inc(S["rstd_done"], 1)
                    seen(pool, "on_ready", 9 * h + c1 + 1)
                    carried(pool, "pool")
                    if c1 >= 2:
                        pool.wait_ge(mix_out[s], 16 * ((5 - s) * h + (c1 - 2) // 2 + 1))
                        carried(pool, "pool")
                    pool.tensor_tensor(mixed[s][:, :], onorm[:, :], pgate[:, :], ALU.add).then_inc(S["sum_done"], 1)
                    seen(pool, "sum_done", 9 * h + c1 + 1)
                    carried(pool, "pool")
                    if c1 < CH:
                        dst, src = mixed_d[c1 * P:(c1 + 1) * P, bass.ds(h * DV, DV)], mixed[s][:, :]
                    else:
                        dst, src = mixed_d[SEQ:NTOK, bass.ds(h * DV, DV)], mixed[s][120:P, :]
                    pool.dma_start(dst, src).then_inc(mix_out[s], 16)
                for s in range(2):
                    pool.wait_ge(mix_out[s], 16 * (5 - s) * (h + 1))
                    carried(pool, "pool")
                assert steps.n == per_head

            with pool.Fori(0, H) as h:
                head(h)
            stage_c_pool(pool, NEWTON + H * per_head)


_INS = ['x_prompt', 'x_sample', 'state_pool', 'state_ret', 'g_mix', 'w_in', 'w_pool', 'pool_scale', 'ret_gn',
        'w_out', 'g_ffn', 'w_grp', 'w_exp', 'w1', 'w3', 'w2', 'g_final']
_OUTS = [(1, SEQ, D), (NB, 1, D), (1, 1, HIST, 512), (1, 1, H, P, DV), (1, NB, HIST, 512), (1, NB, H, P, DV)]


def kernel(**inputs):
    import numpy as _np
    import concourse.bacc as _bacc
    from concourse import mybir as _mybir
    from concourse.bass_utils import run_bass_kernel_spmd as _run

    nc = _bacc.Bacc("TRN2", target_bir_lowering=False, num_devices=1)
    arrays, args = {}, []
    for name in _INS:
        arrays[f"in_{name}_dram"] = _np.ascontiguousarray(inputs[name])
    for name, table in zip(("tables", "head_tables", "masks"), shape_constants()):
        arrays[f"const_{name}_dram"] = table
    for name, a in arrays.items():
        args.append(nc.dram_tensor(name, a.shape, _mybir.dt.from_np(a.dtype), kind="ExternalInput").ap())
    for i, shape in enumerate(_OUTS):
        args.append(nc.dram_tensor(f"out_{i}_dram", shape, _mybir.dt.float32, kind="ExternalOutput").ap())
    step_kernel(nc, *args)
    r = _run(nc, [arrays], core_ids=[0])
    return tuple(r.results[0][f"out_{i}_dram"] for i in range(len(_OUTS)))
```

```python
from contextlib import ExitStack

import numpy as np

import concourse.bass as bass
from concourse import mybir

F32 = mybir.dt.float32
F32R = mybir.dt.float32r
BF16 = mybir.dt.bfloat16
I32 = mybir.dt.int32
ALU = mybir.AluOpType
ACT = mybir.ActivationFunctionType
AX = mybir.AxisListType.X

P = 128
D = 1024
KT = D // P
SEQ, NB, NTOK = 1024, 8, 1032
NT = 9
CH = SEQ // P
TC = NTOK // 3
H = 4
DV = 256
EPS = 1e-6
HIST = 15
SPAN = HIST + SEQ + 16 * NB
LAST = NTOK - P
Q3 = 96
NE, EPG, FE = 32, 8, 256
SPILL = 16
NBLK = NE + SPILL
SLOTS = 3
MAGIC = float(0x5F3759DF)
PAST = 8192
HCW = 2 * P + 16 + 8


def shape_constants():
    half = P // 2
    freqs = (10000.0 ** (-np.arange(half, dtype=np.float64) / half)).astype(np.float32)
    pos = np.concatenate([np.arange(SEQ), np.full(NB, PAST)]).astype(np.float32)
    ang = (pos[:, None] * freqs[None, :]).astype(np.float32).astype(np.float64)
    cs = np.zeros((P, 2, NTOK), np.float32)
    cs[:half, 0] = cs[half:, 0] = np.cos(ang).T
    cs[:half, 1] = np.sin(ang).T
    cs[half:, 1] = -np.sin(ang).T
    log_g = np.log(1.0 - 2.0 ** (-5.0 - np.arange(H)))
    i = np.arange(P)
    scale = P ** -0.5
    hc = np.zeros((P, H, HCW), np.float32)
    for h in range(H):
        d = i[None, :] - i[:, None]
        hc[:, h, 0:P] = np.where(d >= 0, np.exp(np.maximum(d, 0) * log_g[h]), 0.0) * scale
        hc[:, h, P:2 * P] = np.exp((i + 1.0) * log_g[h])[None, :]
        w = 2 << h
        hc[:, h, 2 * P:2 * P + 16] = (w / np.minimum(np.arange(16) + 1, w))[None, :]
        o = 2 * P + 16
        hc[:, h, o + 0] = np.exp((P - 1.0 - i) * log_g[h]) * scale
        hc[:, h, o + 1] = np.exp(P * log_g[h])
        hc[:, h, o + 2] = np.exp(log_g[h])
        hc[:, h, o + 3] = 1.0 / w
        for level in range(1, 4):
            hc[:, h, o + 3 + level] = float(w > (1 << level))
    m = np.zeros((P, MISC), np.float32)
    m[:, IDENT:IDENT + P] = np.eye(P)
    m[:, BEFORE:BEFORE + P] = i[:, None] < i[None, :]
    m[:, ONES:ONES + P] = 1.0
    m[:, IOTA:IOTA + P] = i[None, :]
    m[:, REV:REV + 8] = 8 - np.arange(8)[None, :]
    m[:, THR:THR + 8] = 128.0 * (np.arange(8)[None, :] + 1)
    tok = np.arange(NT)[None, :] * P + i[:, None]
    m[:, PAIR:PAIR + 2 * NT] = 2 * i[:, None] + np.arange(2 * NT)[None, :] % 2
    m[:, TILE:TILE + 2 * NT] = np.arange(2 * NT)[None, :] // 2
    m[:, LIVE:LIVE + 2 * NT] = np.repeat(tok < NTOK, 2, axis=1)
    m[:, QMASK:QMASK + NB * 32] = (np.arange(32)[None, :] == 24 + np.arange(NB)[:, None]).reshape(1, -1)
    m[:, KMASK:KMASK + NB] = i[:, None] == 120 + np.arange(NB)[None, :]
    return cs, hc, m


IDENT, BEFORE, ONES, IOTA = 0, P, 2 * P, 3 * P
REV = 4 * P
THR = REV + 8
PAIR = THR + 8
LIVE = PAIR + 2 * NT
TILE = LIVE + 2 * NT
QMASK = TILE + 2 * NT
KMASK = QMASK + NB * 32
MISC = KMASK + NB


class Region:

    def __init__(self, nc, start, size):
        self.nc, self.at, self.end, self.where = nc, start, start + size, {}

    def place(self, name, shape, dtype):
        t = self.nc.alloc_sbuf_tensor_at(name, list(shape), dtype, offset=self.at)
        self.where[name] = self.at
        self.at += -(-int(np.prod(shape[1:])) * 4 // 32) * 32
        assert self.at <= self.end, (name, self.at - self.end)
        return t


class Steps:

    def __init__(self, eng, sem, carrier=None):
        self.eng, self.sem, self.carrier, self.base, self.n = eng, sem, carrier, 0, 0

    def do(self, ins):
        ins.then_inc(self.sem, 1)
        self.n += 1
        self.eng.wait_ge(self.sem, self.base + self.n)
        if self.carrier is not None:
            self.eng.sem_inc(self.carrier, 1)

    def round_(self, start, index, per):
        self.base, self.n = start + index * per, 0


def newton_rsqrt(steps, eng, x, y, half, t, rounds=3):
    steps.do(eng.tensor_scalar(half, x, -0.5, None, ALU.mult))
    for r in range(rounds):
        steps.do(eng.tensor_tensor(t, y, y, ALU.mult))
        steps.do(eng.tensor_tensor(t, t, half, ALU.mult))
        steps.do(eng.tensor_scalar(t, t, 1.5, None, ALU.add))
        last = eng.tensor_tensor(y, y, t, ALU.mult)
        if r < rounds - 1:
            steps.do(last)
    return last


NEWTON = 12


def rsqrt_guess(steps, eng, x, y, shifted):
    steps.do(eng.tensor_scalar(shifted, x.bitcast(I32), 1, None, ALU.logical_shift_right))
    return eng.tensor_scalar(y.bitcast(I32), shifted, -1.0, MAGIC, ALU.mult, ALU.add)


def step_kernel(nc, x_prompt, x_sample, state_pool, state_ret, g_mix, w_in, w_pool, pool_scale, ret_gn,
                w_out, g_ffn, w_grp, w_exp, w1, w3, w2, g_final, c_cs, c_hc, c_misc,
                y_prompt, y_sample, pool_p, ret_p, pool_s, ret_s):
    w_in = w_in[0].rearrange("(k p) n -> p k n", p=P)
    w_out = w_out[0].rearrange("(k p) n -> p k n", p=P)
    x_p = x_prompt[0]
    x_s = x_sample.rearrange("b o d -> (b o) d")
    mixed_d = nc.dram_tensor("mixed_d", [NTOK, D], F32).ap()
    h2_d = nc.dram_tensor("h2_d", [NTOK, D], F32).ap()
    part_d = nc.dram_tensor("part_d", [2 * NTOK, D], F32).ap()

    with ExitStack() as ctx:
        def sem(name):
            return ctx.enter_context(nc.semaphore(name))

        banks = [ctx.enter_context(nc.psum_tensor(f"bank{i}", [P, 512], F32)) for i in range(8)]

        base = -(-nc.sbuf_base // 32) * 32
        size = (nc.sbuf_top - base) // 32 * 32
        ctx.enter_context(nc.sbuf_tensor("arena", [P, size // 4], F32))
        whole = Region(nc, base, size)
        misc = whole.place("misc", [P, MISC], F32)
        small = whole.place("small", [P, 96], F32)
        bits = whole.place("bits", [P, 32], I32)
        at_hT = whole.at
        hT = [whole.place(n, [P, KT, NTOK], F32R) for n in ("hT_hi", "hT_lo")]
        at_W = whole.at
        wuqk = [whole.place(n, [P, 3, KT, P], F32R) for n in ("wuqk_hi", "wuqk_lo")]
        at_vg = whole.at
        wvg = [whole.place(n, [P, 3, KT, DV], F32R) for n in ("wvg_hi", "wvg_lo")]
        raw = [whole.place(f"raw{i}", [P, 512], F32) for i in range(3)]
        at_small = whole.at

        ra = Region(nc, at_vg, 2 * 3 * KT * DV * 4)
        xall = ra.place("xall", [P, NT, D], F32)
        gmix_b = ra.place("gmix_b", [P, D], F32)
        junk_a = ra.place("junk_a", [P, D], F32)

        rb = Region(nc, at_small, whole.end - at_small)
        cs = rb.place("cs", [P, 2, NTOK], F32)
        hc = rb.place("hc", [P, H, HCW], F32)
        gn_b = rb.place("gn_b", [P, D], F32)
        line = [rb.place(f"line{i}", [P, SPAN + 1], F32) for i in range(3)]
        qT = rb.place("qT", [P, NTOK], F32)
        kT = rb.place("kT", [P, NTOK], F32)
        qx = [rb.place(f"qx{i}", [P, P], F32) for i in range(2)]
        state = rb.place("state", [P, DV], F32)
        sst = [rb.place(f"sample_state{i}", [P, 2, DV], F32) for i in range(2)]
        wp_raw = rb.place("wp_raw", [P, DV], F32)
        wp = rb.place("wp", [P, DV], F32)
        ps_b = rb.place("ps_b", [P, DV], F32)
        vb = [rb.place(f"v{i}", [P, DV], F32) for i in range(2)]
        sg = [rb.place(f"sg{i}", [P, 2 * DV], F32) for i in range(2)]
        sgn = [t[:, DV:2 * DV] for t in sg]
        kz = [rb.place(f"kz{i}", [P, P], F32) for i in range(2)]
        scm = [rb.place(f"scm{i}", [P, P], F32) for i in range(2)]
        onorm = rb.place("onorm", [P, DV], F32)
        pgate = rb.place("pgate", [P, DV], F32)
        mixed = [rb.place(f"mixed{i}", [P, DV], F32) for i in range(2)]
        uout = rb.place("uout", [P, 2, P], F32)
        qm = rb.place("qm", [P, NB, 32], F32)
        ps32 = rb.place("ps32", [P, 32], F32)
        hist = nc.alloc_sbuf_tensor_at("hist", [P, P], F32, offset=rb.where["scm1"])
        kblk = nc.alloc_sbuf_tensor_at("kblk", [P, NB, P], F32, offset=rb.where["line2"])
        rot = nc.alloc_sbuf_tensor_at("rot", [P, TC], F32, offset=rb.where["line2"])

        rh = Region(nc, at_hT, 2 * KT * NTOK * 4)
        x2 = rh.place("x2", [P, NT, D], F32)
        at_rest = rh.at
        mT = [[rh.place(f"mT_{n}{i}", [P, KT, P], F32R) for n in ("hi", "lo")] for i in range(2)]
        mi = [rh.place(f"mixed_in{i}", [P, D], F32) for i in range(2)]
        rw = Region(nc, at_W, 2 * 3 * KT * (P + DV) * 4)
        wo = [[rw.place(f"wo_{n}{k}", [P, D], F32R) for n in ("hi", "lo")] for k in range(KT)]
        wo_raw = [nc.alloc_sbuf_tensor_at(f"wo_raw{k}", [P, D], F32, offset=rw.where[f"wo_lo{k}"])
                  for k in range(3, KT)]
        rc = Region(nc, at_small, whole.end - at_small)
        xr = [rc.place(f"x_again{i}", [P, D], F32) for i in range(2)]
        h2 = [rc.place(f"h2_{i}", [P, D], F32) for i in range(2)]
        h2T = [rc.place(f"h2T{i}", [P, KT, P], F32) for i in range(2)]
        junk_c = rc.place("junk_c", [P, D], F32)
        gffn_b = rc.place("gffn_b", [P, D], F32)
        wr = rc.place("w_router", [P, KT, 36], F32)

        logits = rc.place("logits", [P, NT, 36], F32)
        tmp_e = rc.place("tmp_e", [P, 2 * NT, NE], F32)
        chosen = rc.place("chosen", [P, 2 * NT, NE], F32)
        both = rc.place("both", [P, NT, NE], F32)
        scratch8 = rc.place("scratch8", [P, NT, 8], F32)
        wide8 = rc.place("wide8", [P, NE, 8], F32)
        rc.at = max(rc.at, at_small + 4 * (3 * D + 2 * D + 4 * D + 4 * FE + 5 * FE))
        vec = rc.place("vec", [P, 16, 2 * NT], F32)
        evec = rc.place("evec", [P, 4, NE], F32)
        pair_w = rc.place("pair_w", [P, NT, 2], F32)
        idx_tok = rc.place("idx_tok", [P, NBLK], I32)
        idx_pair = rc.place("idx_pair", [P, NBLK], I32)
        spill = rc.place("spill", [P, 2 * SPILL + 1], I32)
        icol = [rc.place(f"icol{i}", [P, 1], I32) for i in range(SLOTS)]
        jcol = [rc.place(f"jcol{i}", [P, 1], I32) for i in range(SLOTS)]
        both_b = nc.alloc_sbuf_tensor_at("both_b", [P, NT + 1, NE], BF16, offset=rc.at)
        rc.at += (NT + 1) * NE * 2
        count_b = nc.alloc_sbuf_tensor_at("count_b", [P, 2, P], BF16, offset=rc.at)
        rc.at += 2 * P * 2
        assert rc.at <= whole.end
        slot_hot = nc.alloc_sbuf_tensor_at("slot_hot", [P, 2 * NT, P], BF16, offset=rc.where["h2T0"])
        planes = nc.alloc_sbuf_tensor_at("planes", [P, 2 * NT, 3 * NBLK], BF16, offset=at_small - 3 * 2048)

        rm = Region(nc, at_W, 2 * 3 * KT * (P + DV) * 4)
        w13, w2t, w13_lo, w2_lo = [], [], [], []
        for i in range(SLOTS):
            w13.append(rm.place(f"w13_{i}", [P, 2, KT, FE], F32))
            w2t.append(rm.place(f"w2_{i}", [P, 2, D], F32))
            w13_lo.append(nc.alloc_sbuf_tensor_at(f"w13_lo{i}", [P, 2, KT, FE], F32R, offset=rm.where[f"w13_{i}"]))
            w2_lo.append(nc.alloc_sbuf_tensor_at(f"w2_lo{i}", [P, 2, D], F32R, offset=rm.where[f"w2_{i}"]))
        rr = Region(nc, at_rest, at_hT + 2 * KT * NTOK * 4 - at_rest)
        w13_hi = rr.place("w13_hi", [P, KT, 2, FE], F32R)
        w2_hi = rr.place("w2_hi", [P, 4, 512], F32R)
        rx = Region(nc, at_small, whole.end - at_small)
        xg = [rx.place(f"xg{i}", [P, D], F32) for i in range(SLOTS)]
        yb = [rx.place(f"y{i}", [P, D], F32) for i in range(2)]
        xT = [[rx.place(f"xT_{n}{i}", [P, KT, P], F32R) for n in ("hi", "lo")] for i in range(2)]
        aT = [[rx.place(f"aT_{n}{i}", [P, 2, P], F32R) for n in ("hi", "lo")] for i in range(2)]
        sig = [rx.place(f"sig{i}", [P, FE], F32) for i in range(2)]
        act1 = rx.place("act1", [P, FE], F32)
        aa = [rx.place(f"a{i}", [P, FE], F32) for i in range(2)]
        assert rx.at <= rc.where["vec"], (rx.at, rc.where["vec"])

        rf = Region(nc, at_W, 2 * 3 * KT * (P + DV) * 4)
        parts = [rf.place(f"parts{i}", [P, 2, D], F32) for i in range(3)]
        zt = [rf.place(f"z{i}", [P, D], F32) for i in range(3)]
        gfin_b = rf.place("gfin_b", [P, D], F32)
        junk_f = rf.place("junk_f", [P, D], F32)

        SS, MS, RS = 0, 9, 18
        HX, TX = 27, 36
        STAT, MEAN, VAR, GUESS, HALF, TMP, NOW = 48, 54, 55, 56, 57, 58, 60

        ident = misc[:, IDENT:IDENT + P]
        HC0 = 2 * P + 16

        def head_tab(h, a, n):
            return hc[:, bass.ds(h, 1), a:a + n].rearrange("p a b -> p (a b)")

        def head_col(j):
            return small[:, NOW + j:NOW + j + 1]

        const_in = [sem("const_in_a"), sem("const_in_b")]
        x_in = [sem(f"x_in{t}") for t in range(NT)]
        raw_in = [sem(f"raw_in{i}") for i in range(3)]
        misc_in = sem("misc_in")
        ss_in = [sem(f"sample_state_in{i}") for i in range(2)]
        ss_out = [sem(f"sample_state_out{i}") for i in range(2)]
        st_out, u_out, fixed_out = sem("state_out"), sem("u_out"), sem("fixed_out")
        wo_in = [sem(f"w_out_in{k}") for k in range(3, KT)]
        mi_in = [sem(f"mixed_in{i}") for i in range(2)]
        xr_in = [sem(f"x_again_in{i}") for i in range(2)]
        h2_out = [sem(f"h2_out{i}") for i in range(2)]
        route_in = sem("router_weights_in")
        w13_in = [sem(f"w13_in{i}") for i in range(SLOTS)]
        w2_in = [sem(f"w2_in{i}") for i in range(SLOTS)]
        xg_in = [sem(f"xg_in{i}") for i in range(SLOTS)]
        part_out = [sem(f"part_out{i}") for i in range(SLOTS)]
        part_in = [sem(f"part_in{i}") for i in range(3)]
        gfin_in = sem("gfin_in")
        y_out = [sem(f"y_out{i}") for i in range(3)]
        mix_out = [sem(f"mixed_out{i}") for i in range(2)]

        by_pe = {n: sem(n) for n in (
            "xt_mm", "uqk_mm", "g_mm", "v_mm", "kt_mm", "sc_mm", "o_mm", "kv_mm", "skv_mm", "so_mm",
            "ht_mm", "ut_mm", "ct_mm", "w_mm", "t2_mm", "l_mm", "count_mm", "list_mm", "xt2_mm",
            "at_mm", "up_used", "down_used")}
        by_act = {n: sem(n) for n in (
            "sq_done", "h_hi", "w_hi", "u_ev", "hist_ev", "ut_ev", "kz_ev", "v_ev", "sig_done",
            "m_hi", "sq2_done", "h2a_ev", "exp_done", "up_hi", "down_hi", "xT_hi_ev", "sig2_done", "aT_hi_ev",
            "y_ev", "sq3_done",
            "z_done")}
        by_dve = {n: sem(n) for n in (
            "zeroed", "rms_guessed", "normed", "now_ready", "h_lo", "w_lo", "qk_ev", "wp_ready", "pool_ready", "scm_done", "qx_done",
            "state_new", "guess_done", "o_used", "on_ready", "pg_ready", "kblk_done", "qm_done", "s_upd",
            "m_lo", "x2_done", "guess2_done", "h2_done", "h2b_ev", "lg_done", "exp_ready", "chosen_done",
            "hot_done", "routed", "up_lo", "down_lo", "xT_lo_ev", "a_done", "aT_lo_ev", "x3_done",
            "rstd3_done")}
        by_pool = {n: sem(n) for n in (
            "rms_ready", "sgn_done", "rstd_done", "sum_done", "rstd2_done", "gathered_init", "icol_done", "jcol_done",
            "parts_ready", "y_done")}
        by_sp = {n: sem(n) for n in ("head_stored",)}
        S = {**by_pe, **by_act, **by_dve, **by_pool, **by_sp}
        steps_dve, steps_f, steps_pool = sem("steps_dve"), sem("steps_f"), sem("steps_pool")
        carrier = {n: sem(f"carry_{n}") for n in ("pool", "sp", "dve")}

        def begin(eng, own):
            for s in own.values():
                eng.sem_inc(s, 1)

        def after(n):
            return max(n, 0) + 1 if isinstance(n, int) else n + 1

        def carried(eng, who):
            eng.sem_inc(carrier[who], 1)

        block = ctx.enter_context(nc.Block())

        def piece(q, h):
            if q < 6:
                j, k = q // 2, 4 * (q % 2)
                col = (0, 512, 1024)[j] + h * P
                return w_in[:, k:k + 4, bass.ds(col, P)], [w[:, j, k:k + 4, :] for w in wuqk], (4, P)
            j, k = (q - 6) // 4, 2 * ((q - 6) % 4)
            col = (1536, 2560, 3584)[j] + h * DV
            return w_in[:, k:k + 2, bass.ds(col, DV)], [w[:, j, k:k + 2, :] for w in wvg], (2, DV)

        def load_piece(eng, q, h, n):
            eng.wait_ge(S["w_lo"], after(n - 2))
            src, _, (k, w) = piece(q, h)
            eng.dma_start(raw[q % 3][:, :].rearrange("p (k n) -> p k n", k=k), src).then_inc(raw_in[q % 3], 16)

        def slot_count(h, q):
            return 16 * (6 * h + q // 3 + 1)

        def tiles(eng, step):
            step(0, 0)
            step(1, 1)
            with eng.Fori(1, CH // 2) as i:
                for s in range(2):
                    step(2 * i + s, s)
            step(CH, 0)

        def is_first(t, n):
            return isinstance(t, int) and t < n

        def row_tile(buf, t):
            return buf[:, t, :] if isinstance(t, int) else buf[:, bass.ds(t, 1), :].rearrange("p a n -> p (a n)")

        WOUT0 = 18 * H

        def load_wout(eng, q):
            eng.wait_ge(S["w_lo"], after(WOUT0 + q - 2))
            eng.dma_start(raw[q % 3][:, :], w_out[:, q // 2, (q % 2) * 512:(q % 2 + 1) * 512])\
                .then_inc(raw_in[q % 3], 16)

        def load_wout_rest(eng):
            for k in range(3, KT):
                eng.dma_start(wo_raw[k - 3][:, :], w_out[:, k, :]).then_inc(wo_in[k - 3], 16)

        def round_wout_rest(act):
            for k in range(3, KT):
                act.wait_ge(wo_in[k - 3], 16)
                act.activation(wo[k][0][:, :], wo_raw[k - 3][:, :], ACT.Copy).then_inc(S["w_hi"], 1)

        def low_wout_rest(dve, i):
            for k in (3 + i,) if i < 3 else (6, 7):
                dve.wait_ge(S["w_hi"], after(WOUT0 + 6 + k - 2))
                dve.tensor_tensor(wo[k][1][:, :], wo_raw[k - 3][:, :], wo[k][0][:, :], ALU.subtract)\
                    .then_inc(S["w_lo"], 1)

        def wout_half(q, which):
            return wo[q // 2][which][:, (q % 2) * 512:(q % 2 + 1) * 512]

        def round_wout(act, q):
            act.wait_ge(raw_in[q % 3], 16 * (WOUT0 // 3 + q // 3 + 1))
            act.activation(wout_half(q, 0), raw[q % 3][:, :], ACT.Copy).then_inc(S["w_hi"], 1)

        def low_wout(dve, q):
            dve.tensor_tensor(wout_half(q, 1), raw[q % 3][:, :], wout_half(q, 0), ALU.subtract)\
                .then_inc(S["w_lo"], 1)

        def of_expert(w, e):
            return w[0, e] if isinstance(e, int) else w[0, bass.ds(e, 1)].rearrange("a d f -> (a d) f")

        def up_weights(sp, e, s):
            for j, w in enumerate((w1, w3)):
                sp.dma_start(w13[s][:, j, :, :].rearrange("p k f -> p (k f)"),
                             of_expert(w, e).rearrange("(p k) f -> p (k f)", p=P)).then_inc(w13_in[s], 16)

        def down_weights(sp, e, s):
            sp.dma_start(w2t[s][:, :, :].rearrange("p i n -> p (i n)"),
                         of_expert(w2, e).rearrange("(p i) n -> p (i n)", p=P)).then_inc(w2_in[s], 16)

        ROUND = 2 * SLOTS
        ROUNDS = NE // ROUND

        def blocks(eng, step):
            for s in range(ROUND):
                step(s, s, 0)
            with eng.Fori(1, ROUNDS) as g:
                for s in range(ROUND):
                    step(ROUND * g + s, s, g)
            for s in range(NE - ROUND * ROUNDS):
                step(ROUND * ROUNDS + s, s, ROUNDS)

        def uses(s, g):
            return 2 * g + s // SLOTS + 1

        MAIN_USES = [len(range(s, NE, SLOTS)) for s in range(SLOTS)]

        def up_piece(s, k):
            return w13[s][:, :, k, :], w13_hi[:, k, :, :], w13_lo[s][:, :, k, :]

        def down_piece(s, j):
            at = (slice(None), j % 2, slice(j // 2 * 512, (j // 2 + 1) * 512))
            return w2t[s][at], w2_hi[:, j, :], w2_lo[s][at]

        def spilled(eng, step):
            many = eng.value_load(spill[0:1, 2 * SPILL:2 * SPILL + 1], min_val=0, max_val=SPILL)
            with eng.If(many > 0):
                with eng.Fori(0, SPILL) as i:
                    live = eng.value_load(spill[0:1, bass.ds(i, 1)], min_val=0, max_val=1)
                    with eng.If(live > 0):
                        step(NE + i, i)
                    eng.nop()
                eng.nop()

        def load_mixed(sp, t, s):
            if not is_first(t, 2):
                sp.wait_ge(S["ct_mm"], after(2 * (t - 1)))
                if not isinstance(t, int):
                    carried(sp, "sp")
            sp.wait_ge(mix_out[s], 16 * ((5 - s) * (H - 1) + 1) + (16 * (t // 2) if isinstance(t, int)
                                                                  else 8 * (t - s)))
            if not isinstance(t, int):
                carried(sp, "sp")
            if isinstance(t, int) and t == CH:
                sp.dma_start(mi[s][0:NB, :], mixed_d[SEQ:NTOK, :]).then_inc(mi_in[s], 16)
            else:
                sp.dma_start(mi[s][:, :], mixed_d[bass.ds(t * P, P), :]).then_inc(mi_in[s], 16)

        def load_x(sp, t, s):
            if not is_first(t, 2):
                sp.wait_ge(S["x2_done"], after(2 * (t - 1)))
                if not isinstance(t, int):
                    carried(sp, "sp")
            if isinstance(t, int) and t == CH:
                sp.dma_start(xr[s][0:NB, :], x_s).then_inc(xr_in[s], 16)
            else:
                sp.dma_start(xr[s][:, :], x_p[bass.ds(t * P, P), :]).then_inc(xr_in[s], 16)

        def first_loads_c(sp, i):
            if i == 0:
                sp.wait_ge(S["v_mm"], after(9 * H))
                load_wout_rest(sp)
            elif i == 1:
                sp.wait_ge(S["qk_ev"], after(6 * H))
                load_mixed(sp, 0, 0)
                load_x(sp, 0, 0)
                load_mixed(sp, 1, 1)

        def stage_c_sp(sp):
            sp.wait_ge(S["sum_done"], after(9 * H))
            sp.dma_start(gffn_b[:, :], g_ffn[0:1, :].to_broadcast([P, D])).then_inc(route_in, 16)
            sp.dma_start(wr[:, :, 0:4], w_grp[0].rearrange("(k p) g -> p k g", p=P)).then_inc(route_in, 16)
            sp.dma_start(wr[:, :, 4:36], w_exp[0].rearrange("(k p) g e -> p k (g e)", p=P))\
                .then_inc(route_in, 16)
            with sp.Fori(1, CH // 2) as i:
                for s in range(2):
                    load_mixed(sp, 2 * i + s, s)
                    load_x(sp, 2 * i + s - 1, 1 - s)
            load_mixed(sp, CH, 0)
            load_x(sp, CH - 1, 1)
            load_x(sp, CH, 0)

            def weights(b, s, g):
                if not is_first(b, SLOTS):
                    sp.wait_ge(S["up_used"], after(KT * (b - SLOTS + 1)))
                    if not isinstance(b, int):
                        carried(sp, "sp")
                up_weights(sp, b, s % SLOTS)
                if is_first(b, 1):
                    return
                if not is_first(b, SLOTS + 1):
                    sp.wait_ge(S["down_used"], after(4 * (b - SLOTS)))
                    if not isinstance(b, int):
                        carried(sp, "sp")
                down_weights(sp, b - 1, (s - 1) % SLOTS)

            sp.wait_ge(S["w_mm"], after(NT))
            blocks(sp, weights)
            sp.wait_ge(S["down_used"], after(4 * (NE - SLOTS)))
            down_weights(sp, NE - 1, (NE - 1) % SLOTS)
            sp.wait_ge(S["routed"], after(1))

            def more(b, i):
                sp.wait_ge(S["down_used"], after(4 * b))
                carried(sp, "sp")
                e = sp.value_load(spill[0:1, bass.ds(i + SPILL, 1)], min_val=0, max_val=NE - 1)
                up_weights(sp, e, 0)
                down_weights(sp, e, 0)

            spilled(sp, more)

            sp.wait_ge(S["parts_ready"], after(1))
            for t in range(NT):
                rows = P if t < CH else NB
                sp.wait_ge(S["x3_done"], after(t - 2))
                sp.dma_start(parts[t % 3][0:rows, :, :].rearrange("p j n -> p (j n)"),
                             part_d[2 * t * P:2 * (t * P + rows), :].rearrange("(p j) n -> p (j n)", j=2))\
                    .then_inc(part_in[t % 3], 16)
                if t == 1:
                    sp.dma_start(gfin_b[:, :], g_final.unsqueeze(0).to_broadcast([P, D])).then_inc(gfin_in, 16)
            for t in range(NT):
                rows = P if t < CH else NB
                dst = y_prompt[0, t * P:(t + 1) * P, :] if t < CH else y_sample.rearrange("b o d -> (b o) d")
                sp.wait_ge(S["y_done"], after(t + 1))
                sp.dma_start(dst, zt[t % 3][0:rows, :]).then_inc(y_out[t % 3], 16)
            for s in range(3):
                sp.wait_ge(y_out[s], 16 * 3)

        def stage_c_act(act):
            act.wait_ge(S["v_mm"], after(9 * H))
            round_wout_rest(act)

            def high(t, s):
                for b in range(2):
                    act.wait_ge(S["ct_mm"], after(2 * t + b + 1))
                    act.wait_ge(S["w_mm"], after(t - 1))
                    act.activation(mT[s][0][:, 4 * b:4 * b + 4, :].rearrange("p k n -> p (k n)"), banks[b][:, :],
                                   ACT.Copy).then_inc(S["m_hi"], 1)

            def h2_out_of_psum(t, s):
                act.wait_ge(S["t2_mm"], after(2 * t + 1))
                act.wait_ge(S["l_mm"], after(t - 1))
                act.activation(h2T[s][:, 0:4, :].rearrange("p k n -> p (k n)"), banks[6][:, :], ACT.Copy)\
                    .then_inc(S["h2a_ev"], 1)

            def step(t, s):
                if not (isinstance(t, int) and t == CH):
                    high(t + 1, 1 - s)
                if not is_first(t, 1):
                    h2_out_of_psum(t - 1, 1 - s)
                act.wait_ge(S["x2_done"], after(2 * t + 2))
                act.wait_ge(S["sq2_done"], after(t))
                act.wait_ge(S["h2_done"], after(t - 1))
                act.activation(junk_c[:, :], row_tile(x2, t), ACT.Square,
                               accum_out=small[:, SS + s:SS + s + 1]).then_inc(S["sq2_done"], 1)

            high(0, 0)
            tiles(act, step)
            h2_out_of_psum(CH, 0)
            act.wait_ge(S["exp_ready"], after(1))
            act.activation(tmp_e[:, 0:NT, 0:4], tmp_e[:, 0:NT, 4:8], ACT.Exp).then_inc(S["exp_done"], 1)
            act.wait_ge(S["exp_ready"], after(2))
            act.activation(vec[:, 6, 0:NT], vec[:, 5, 0:NT], ACT.Exp).then_inc(S["exp_done"], 1)

            def up_high(b, s, g, k):
                if k == 0:
                    act.wait_ge(w13_in[s % SLOTS], 32 * uses(s, g))
                if not is_first(b, 1):
                    act.wait_ge(S["up_used"], after(KT * (b - 1) + k + 1))
                whole_w, hi, _ = up_piece(s % SLOTS, k)
                act.activation(hi, whole_w, ACT.Copy).then_inc(S["up_hi"], 1)

            def down_high(b, slot, used, j):
                if j == 0:
                    act.wait_ge(w2_in[slot], 16 * used)
                act.wait_ge(S["down_used"], after(4 * (b - 1) + j + 1))
                whole_w, hi, _ = down_piece(slot, j)
                act.activation(hi, whole_w, ACT.Copy).then_inc(S["down_hi"], 1)

            def x_high(b, s2):
                for n in range(2):
                    act.wait_ge(S["xt2_mm"], after(2 * b + n + 1))
                    if n == 0:
                        act.wait_ge(S["up_used"], after(KT * (b - 1)))
                    act.activation(xT[s2][0][:, 4 * n:4 * n + 4, :].rearrange("p k n -> p (k n)"), banks[n][:, :],
                                   ACT.Copy).then_inc(S["xT_hi_ev"], 1)

            def sigmoid(b, s2):
                act.wait_ge(S["up_used"], after(KT * (b + 1)))
                act.wait_ge(S["a_done"], after(b - 1))
                act.activation(sig[s2][:, :], banks[2 + s2][:, 0:FE], ACT.Sigmoid).then_inc(S["sig2_done"], 1)

            def a_high(b, s2):
                act.wait_ge(S["at_mm"], after(b + 1))
                act.wait_ge(S["down_used"], after(4 * (b - 1)))
                act.activation(aT[s2][0][:, :, :].rearrange("p i n -> p (i n)"), banks[4][:, 0:2 * P], ACT.Copy)\
                    .then_inc(S["aT_hi_ev"], 1)

            def y_out_of_psum(b, s2):
                act.wait_ge(S["down_used"], after(4 * (b + 1)))
                for n in range(2):
                    act.activation(yb[s2][:, n * 512:(n + 1) * 512], banks[5 + n][:, :], ACT.Copy)\
                        .then_inc(S["y_ev"], 1)

            def y_stored(b, s, g):
                if not is_first(b, 2):
                    act.wait_ge(part_out[(s - 2) % SLOTS], 16 * uses(s - 2, g))

            def step_m(b, s, g):
                last = isinstance(b, int) and b == NE - 1
                if not last:
                    for k in range(6):
                        up_high(b + 1, s + 1, g, k)
                sigmoid(b, s % 2)
                if not last:
                    for k in range(6, KT):
                        up_high(b + 1, s + 1, g, k)
                    x_high(b + 1, (s + 1) % 2)
                if not is_first(b, 1):
                    y_stored(b - 1, s - 1, g)
                    y_out_of_psum(b - 1, (s - 1) % 2)
                a_high(b, s % 2)
                for j in range(4):
                    down_high(b, s % SLOTS, uses(s, g), j)

            for k in range(KT):
                up_high(0, 0, 0, k)
            x_high(0, 0)
            blocks(act, step_m)
            y_stored(NE - 1, (NE - 1) % ROUND, ROUNDS)
            y_out_of_psum(NE - 1, (NE - 1) % 2)

            def more(b, i):
                act.wait_ge(w13_in[0], 32 * (MAIN_USES[0] + i + 1))
                for k in range(KT):
                    act.wait_ge(S["up_used"], after(KT * (b - 1) + k + 1))
                    whole_w, hi, _ = up_piece(0, k)
                    act.activation(hi, whole_w, ACT.Copy).then_inc(S["up_hi"], 1)
                x_high(b, 0)
                sigmoid(b, 0)
                a_high(b, 0)
                for j in range(4):
                    down_high(b, 0, MAIN_USES[0] + i + 1, j)
                for s in range(1, SLOTS):
                    act.wait_ge(part_out[s], 16 * MAIN_USES[s])
                act.wait_ge(part_out[0], 16 * (MAIN_USES[0] + i))
                y_out_of_psum(b, 0)

            spilled(act, more)

            act.wait_ge(S["parts_ready"], after(1))
            for t in range(NT):
                act.wait_ge(S["x3_done"], after(t + 1))
                act.wait_ge(S["sq3_done"], after(t))
                act.activation(junk_f[:, :], x2[:, t, :], ACT.Square, accum_out=small[:, SS + t:SS + t + 1])\
                    .then_inc(S["sq3_done"], 1)
                for u in ready_by(t):
                    act.wait_ge(S["rstd3_done"], after(u // 3 + 1))
                    if u >= 3:
                        act.wait_ge(y_out[u % 3], 16 * (u // 3))
                    act.activation(zt[u % 3][:, :], x2[:, u, :], ACT.Identity, scale=small[:, RS + u:RS + u + 1])\
                        .then_inc(S["z_done"], 1)

        def ready_by(t):
            return {2: (), 5: (0, 1, 2), 8: (3, 4, 5, 6, 7, 8)}.get(t, ())

        def three(pe, out, lhs, rhs, first, last):
            pe.matmul(out, lhs[0], rhs[0], start=first, stop=False)
            pe.matmul(out, lhs[0], rhs[1], start=False, stop=False)
            return pe.matmul(out, lhs[1], rhs[0], start=False, stop=last)

        def stage_c_pe(pe, last_samples):
            for n in range(3):
                last_samples(n)
            pe.wait_ge(S["sig_done"], after(9 * H))
            pe.wait_ge(S["kz_ev"], after(9 * H))

            def mixed_over(t, s):
                for b in range(2):
                    if b == 0:
                        pe.wait_ge(mi_in[s], 16 * (t // 2 + 1) if isinstance(t, int) else 8 * (t - s) + 16)
                    pe.wait_ge(S["m_lo"], after(2 * (t - 1) + b + 1))
                    for j in range(4):
                        mm = pe.transpose(banks[b][:, j * P:(j + 1) * P], mi[s][:, (4 * b + j) * P:(4 * b + j + 1) * P],
                                          ident)
                    mm.then_inc(S["ct_mm"], 1)

            def out_product(t, s):
                pe.wait_ge(S["m_lo"], after(2 * t + 2))
                pe.wait_ge(S["x2_done"], after(2 * (t - 1)))
                if is_first(t, 1):
                    pe.wait_ge(S["w_lo"], after(WOUT0 + 6 + KT - 3))
                for k in range(KT):
                    for xi, wi in ((0, 0), (0, 1), (1, 0)):
                        for n in range(2):
                            mm = pe.matmul(banks[2 + 2 * s + n][:, :], mT[s][xi][:, k, :],
                                           wo[k][wi][:, n * 512:(n + 1) * 512], start=(k == 0 and xi + wi == 0),
                                           stop=(k == KT - 1 and xi == 1))
                mm.then_inc(S["w_mm"], 1)

            def h2_over(t, s):
                pe.wait_ge(S["h2_done"], after(t + 1))
                for b in range(2):
                    pe.wait_ge(S["lg_done" if b == 0 else "h2b_ev"], after(t))
                    for j in range(4):
                        k = 4 * b + j
                        mm = pe.transpose(banks[6 + b][:, j * P:(j + 1) * P], h2[s][:, k * P:(k + 1) * P], ident)
                    mm.then_inc(S["t2_mm"], 1)

            def router(t, s):
                pe.wait_ge(S["h2a_ev"], after(t + 1))
                pe.wait_ge(S["h2b_ev"], after(t + 1))
                if is_first(t, 1):
                    pe.wait_ge(route_in, 48)
                for k in range(KT):
                    mm = pe.matmul(banks[6][:, 0:36], h2T[s][:, k, :], wr[:, k, :], start=(k == 0),
                                   stop=(k == KT - 1))
                mm.then_inc(S["l_mm"], 1)

            def step(t, s):
                if not (isinstance(t, int) and t == CH):
                    mixed_over(t + 1, 1 - s)
                if not is_first(t, 2):
                    router(t - 2, s)
                out_product(t, s)
                if not is_first(t, 1):
                    h2_over(t - 1, 1 - s)

            mixed_over(0, 0)
            for n in range(3, 5):
                last_samples(n)
            tiles(pe, step)
            router(CH - 1, 1)
            h2_over(CH, 0)
            router(CH, 0)

            pe.wait_ge(S["chosen_done"], after(1))
            table = banks[0][:, 0:(NT + 1) * NE].rearrange("p (t e) -> p t e", e=NE)
            pe.matmul(table, count_b[:, 0, :], both_b[:, :, :], start=True, stop=False)
            for t in reversed(range(NT)):
                mm = pe.matmul(table[:, t + 1:NT + 1, :], count_b[:, 1, :],
                               both_b[:, t:t + 1, :].to_broadcast([P, NT - t, NE]), start=False, stop=(t == 0))
            mm.then_inc(S["count_mm"], 1)
            pe.wait_ge(S["hot_done"], after(1))
            for i in range(2 * NT):
                mm = pe.matmul(banks[2][:, 0:3 * NBLK], slot_hot[:, i, :], planes[:, i, :], start=(i == 0),
                               stop=(i == 2 * NT - 1))
            mm.then_inc(S["list_mm"], 1)

            def x_over(b, slot, used):
                pe.wait_ge(xg_in[slot], 16 * used)
                view = xg[slot][:, :].rearrange("p (d k) -> p k d", k=KT)
                for n in range(2):
                    pe.wait_ge(S["xT_lo_ev"], after(2 * (b - 1) + n + 1))
                    for j in range(4):
                        mm = pe.transpose(banks[n][:, j * P:(j + 1) * P], view[:, 4 * n + j, :], ident)
                    mm.then_inc(S["xt2_mm"], 1)

            def up(b, slot, s2):
                pe.wait_ge(S["a_done"], after(b - 1))
                out = banks[2 + s2][:, :].rearrange("p (j f) -> p j f", j=2)
                for k in range(KT):
                    if k % 4 == 0:
                        pe.wait_ge(S["xT_lo_ev"], after(2 * b + k // 4 + 1))
                    pe.wait_ge(S["up_lo"], after(KT * b + k + 1))
                    _, hi, lo = up_piece(slot, k)
                    mm = three(pe, out, [t[:, k, :] for t in xT[s2]], [hi, lo], k == 0, k == KT - 1)
                    mm.then_inc(S["up_used"], 1)

            def a_over(b, s2):
                pe.wait_ge(S["a_done"], after(b + 1))
                pe.wait_ge(S["aT_lo_ev"], after(b))
                view = aa[s2][:, :].rearrange("p (f i) -> p i f", i=2)
                for i in range(2):
                    mm = pe.transpose(banks[4][:, i * P:(i + 1) * P], view[:, i, :], ident)
                mm.then_inc(S["at_mm"], 1)

            def down(b, slot, s2):
                pe.wait_ge(S["aT_lo_ev"], after(b + 1))
                pe.wait_ge(S["y_ev"], after(2 * b))
                for j in range(4):
                    pe.wait_ge(S["down_lo"], after(4 * b + j + 1))
                    _, hi, lo = down_piece(slot, j)
                    mm = three(pe, banks[5 + j // 2][:, :], [t[:, j % 2, :] for t in aT[s2]], [hi, lo], j % 2 == 0,
                               j % 2 == 1)
                    mm.then_inc(S["down_used"], 1)

            def step_m(b, s, g):
                up(b, s % SLOTS, s % 2)
                if not (isinstance(b, int) and b == NE - 1):
                    x_over(b + 1, (s + 1) % SLOTS, uses(s + 1, g))
                if not is_first(b, 1):
                    down(b - 1, (s - 1) % SLOTS, (s - 1) % 2)
                a_over(b, s % 2)

            x_over(0, 0, 1)
            blocks(pe, step_m)
            down(NE - 1, (NE - 1) % SLOTS, (NE - 1) % 2)
            pe.wait_ge(S["routed"], after(1))

            def more(b, i):
                x_over(b, 0, MAIN_USES[0] + i + 1)
                up(b, 0, 0)
                a_over(b, 0)
                down(b, 0, 0)

            spilled(pe, more)

        def low_mixed(dve, t, s):
            for b in range(2):
                dve.wait_ge(S["m_hi"], after(2 * t + b + 1))
                at = (slice(None), slice(4 * b, 4 * b + 4), slice(None))
                dve.tensor_tensor(mT[s][1][at].rearrange("p k n -> p (k n)"), banks[b][:, :],
                                  mT[s][0][at].rearrange("p k n -> p (k n)"), ALU.subtract)\
                    .then_inc(S["m_lo"], 1)

        def stage_c_dve(dve, done):
            steps = Steps(dve, steps_dve)
            def logits_out(t):
                dve.wait_ge(S["l_mm"], after(t + 1))
                dve.tensor_copy(row_tile(logits, t), banks[6][:, 0:36]).then_inc(S["lg_done"], 1)

            def h2_out_of_psum(t, s):
                dve.wait_ge(S["t2_mm"], after(2 * t + 2))
                dve.wait_ge(S["l_mm"], after(t - 1))
                dve.tensor_copy(h2T[s][:, 4:8, :].rearrange("p k n -> p (k n)"), banks[7][:, :])\
                    .then_inc(S["h2b_ev"], 1)

            def step(t, s, start, index):
                steps.round_(start, index, 4)
                steps.n = 2 * s
                if not (isinstance(t, int) and t == CH):
                    low_mixed(dve, t + 1, 1 - s)
                if not is_first(t, 2):
                    logits_out(t - 2)
                dve.wait_ge(S["w_mm"], after(t + 1))
                dve.wait_ge(xr_in[s], 16 * (t // 2 + 1) if isinstance(t, int) else 8 * (t - s) + 16)
                dst = row_tile(x2, t)
                for n in range(2):
                    half = slice(n * 512, (n + 1) * 512)
                    dve.tensor_tensor(dst[:, half], banks[2 + 2 * s + n][:, :], xr[s][:, half], ALU.add)\
                        .then_inc(S["x2_done"], 1)
                if not is_first(t, 1):
                    h2_out_of_psum(t - 1, 1 - s)
                ms, rs = small[:, MS + s:MS + s + 1], small[:, RS + s:RS + s + 1]
                dve.wait_ge(S["sq2_done"], after(t + 1))
                steps.do(dve.tensor_scalar(ms, small[:, SS + s:SS + s + 1], 1.0 / D, EPS, ALU.mult, ALU.add))
                rsqrt_guess(steps, dve, ms, rs, bits[:, 0:1]).then_inc(S["guess2_done"], 1)
                dve.wait_ge(S["rstd2_done"], after(t + 1))
                dve.wait_ge(S["t2_mm"], after(2 * (t - 1)))
                if not is_first(t, 2):
                    dve.wait_ge(h2_out[s], 16 * (t // 2) if isinstance(t, int) else 8 * (t - s))
                dve.scalar_tensor_tensor(out=h2[s][:, :], in0=dst, scalar=rs, in1=gffn_b[:, :],
                                         op0=ALU.mult, op1=ALU.mult).then_inc(S["h2_done"], 1)

            dve.wait_ge(route_in, 48)
            dve.tensor_copy(count_b[:, :, :].rearrange("p a n -> p (a n)"), misc[:, BEFORE:BEFORE + 2 * P])
            dve.memset(both_b[:, NT, :], 0.0)
            step(0, 0, done, 0)
            step(1, 1, done, 0)
            with dve.Fori(1, CH // 2) as i:
                for s in range(2):
                    step(2 * i + s, s, done, i)
            step(CH, 0, done, CH // 2)
            logits_out(CH - 1)
            h2_out_of_psum(CH, 0)
            logits_out(CH)

            steps.base, steps.n = done + 4 * (CH // 2) + 2, 0
            dve.wait_ge(S["lg_done"], after(NT))
            route(dve, steps)

            start = steps.base + steps.n

            def up_low(b, slot, k):
                dve.wait_ge(S["up_hi"], after(KT * b + k + 1))
                whole_w, hi, lo = up_piece(slot, k)
                dve.tensor_tensor(lo, whole_w, hi, ALU.subtract).then_inc(S["up_lo"], 1)

            def down_low(b, slot, j):
                dve.wait_ge(S["down_hi"], after(4 * b + j + 1))
                whole_w, hi, lo = down_piece(slot, j)
                dve.tensor_tensor(lo, whole_w, hi, ALU.subtract).then_inc(S["down_lo"], 1)

            def x_low(b, s2):
                for n in range(2):
                    dve.wait_ge(S["xT_hi_ev"], after(2 * b + n + 1))
                    hi, lo = (t[:, 4 * n:4 * n + 4, :].rearrange("p k n -> p (k n)") for t in xT[s2])
                    dve.tensor_tensor(lo, banks[n][:, :], hi, ALU.subtract).then_inc(S["xT_lo_ev"], 1)

            def gate(b, s2):
                steps.round_(start, b, 1)
                dve.wait_ge(S["sig2_done"], after(b + 1))
                dve.wait_ge(S["a_done"], after(b))
                steps.do(dve.tensor_tensor(act1[:, :], banks[2 + s2][:, 0:FE], sig[s2][:, :], ALU.mult))
                dve.wait_ge(S["at_mm"], after(b - 1))
                dve.tensor_tensor(aa[s2][:, :], banks[2 + s2][:, FE:2 * FE], act1[:, :], ALU.mult)\
                    .then_inc(S["a_done"], 1)

            def a_low(b, s2):
                dve.wait_ge(S["aT_hi_ev"], after(b + 1))
                hi, lo = (t[:, :, :].rearrange("p i n -> p (i n)") for t in aT[s2])
                dve.tensor_tensor(lo, banks[4][:, 0:2 * P], hi, ALU.subtract).then_inc(S["aT_lo_ev"], 1)

            def step_m(b, s, g):
                last = isinstance(b, int) and b == NE - 1
                if not last:
                    for k in range(6):
                        up_low(b + 1, (s + 1) % SLOTS, k)
                gate(b, s % 2)
                if not last:
                    for k in range(6, KT):
                        up_low(b + 1, (s + 1) % SLOTS, k)
                    x_low(b + 1, (s + 1) % 2)
                a_low(b, s % 2)
                for j in range(4):
                    down_low(b, s % SLOTS, j)

            for k in range(KT):
                up_low(0, 0, k)
            x_low(0, 0)
            blocks(dve, step_m)

            def more(b, i):
                for k in range(KT):
                    up_low(b, 0, k)
                x_low(b, 0)
                gate(b, 0)
                a_low(b, 0)
                for j in range(4):
                    down_low(b, 0, j)

            spilled(dve, more)

            dve.wait_ge(S["parts_ready"], after(1))
            many = Steps(dve, steps_f)

            def add_parts(t):
                dve.wait_ge(part_in[t % 3], 16 * (t // 3 + 1))
                many.do(dve.scalar_tensor_tensor(out=x2[:, t, :], in0=parts[t % 3][:, 0, :], scalar=pair_w[:, t, 0:1],
                                                 in1=x2[:, t, :], op0=ALU.mult, op1=ALU.add))
                dve.scalar_tensor_tensor(out=x2[:, t, :], in0=parts[t % 3][:, 1, :], scalar=pair_w[:, t, 1:2],
                                         in1=x2[:, t, :], op0=ALU.mult, op1=ALU.add).then_inc(S["x3_done"], 1)

            def norms(r):
                dve.wait_ge(S["sq3_done"], after(3 * r + 3))
                a, b = 3 * r, 3 * r + 3
                many.do(dve.tensor_scalar(small[:, MS + a:MS + b], small[:, SS + a:SS + b], 1.0 / D, EPS,
                                          ALU.mult, ALU.add))
                many.do(rsqrt_guess(many, dve, small[:, MS + a:MS + b], small[:, RS + a:RS + b], bits[:, a:b]))
                newton_rsqrt(many, dve, small[:, MS + a:MS + b], small[:, RS + a:RS + b], small[:, HX + a:HX + b],
                             small[:, TX + a:TX + b]).then_inc(S["rstd3_done"], 1)

            for t in range(NT):
                add_parts(t)
                if t in (3, 6):
                    norms(t // 3 - 1)
            norms(2)

        def route(dve, st):
            do = st.do
            rev8 = misc[:, REV:REV + 8].unsqueeze(1).to_broadcast([P, NT, 8])
            rev4 = misc[:, REV + 4:REV + 8].unsqueeze(1).to_broadcast([P, NT, 4])
            live = misc[:, LIVE:LIVE + 2 * NT]
            iota = misc[:, IOTA:IOTA + P]
            lg, le4 = logits[:, :, 0:4], logits[:, :, 4:36].rearrange("p t (g e) -> p t g e", g=4)
            top, rank, total, m1, m2, d12, e12, pg = (vec[:, i, 0:NT] for i in range(8))
            pos, q, rem, exp_id, adj, blk = (vec[:, i, :] for i in range(8, 14))
            rank1, rank2 = vec[:, 14, 0:NT], vec[:, 14, NT:2 * NT]
            goh, eq4, d4 = tmp_e[:, 0:NT, 8:12], tmp_e[:, 0:NT, 12:16], tmp_e[:, 0:NT, 4:8]
            le, oh1, oh2 = both[:, :, 0:8], both[:, :, 8:16], both[:, :, 16:24]
            le2, eq8 = both[:, :, 24:32], scratch8[:, :, :]

            def along(v, n):
                return v.unsqueeze(2).to_broadcast([P, v.shape[1], n])

            def pick(values, hot, scratch, best, first, rev, n):
                do(dve.tensor_reduce(best, values, AX, ALU.max))
                do(dve.tensor_tensor(scratch, values, along(best, n), ALU.is_equal))
                do(dve.tensor_tensor(scratch, scratch, rev, ALU.mult))
                do(dve.tensor_reduce(first, scratch, AX, ALU.max))
                do(dve.tensor_tensor(hot, rev, along(first, n), ALU.is_equal))

            pick(lg, goh, eq4, top, rank, rev4, 4)
            do(dve.tensor_tensor(d4, lg, along(top, 4), ALU.subtract))
            dve.sem_inc(S["exp_ready"], 1)
            wide = chosen[:, 0:NT, :].rearrange("p t (g e) -> p t g e", g=4)
            do(dve.tensor_tensor(wide, le4, goh.unsqueeze(3).to_broadcast([P, NT, 4, 8]), ALU.mult))
            do(dve.tensor_reduce(le, wide.rearrange("p t g e -> p t e g"), AX, ALU.add))
            pick(le, oh1, eq8, m1, rank1, rev8, 8)
            do(dve.scalar_tensor_tensor(out=le2, in0=oh1, scalar=-3e38, in1=le, op0=ALU.mult, op1=ALU.add))
            pick(le2, oh2, eq8, m2, rank2, rev8, 8)
            do(dve.tensor_tensor(d12, m2, m1, ALU.subtract))
            dve.sem_inc(S["exp_ready"], 1)
            do(dve.tensor_tensor(goh, goh, along(live[:, 0:2 * NT:2], 4), ALU.mult))
            for j, hot in enumerate((oh1, oh2)):
                do(dve.tensor_tensor(chosen[:, j:2 * NT:2, :].rearrange("p t (g e) -> p t g e", g=4),
                                     goh.unsqueeze(3).to_broadcast([P, NT, 4, 8]),
                                     hot.unsqueeze(2).to_broadcast([P, NT, 4, 8]), ALU.mult))
            dve.tensor_tensor(both_b[:, 0:NT, :], chosen[:, 0:2 * NT:2, :], chosen[:, 1:2 * NT:2, :], ALU.add)\
                .then_inc(S["chosen_done"], 1)
            dve.wait_ge(S["exp_done"], after(2))
            do(dve.tensor_reduce(total, tmp_e[:, 0:NT, 0:4], AX, ALU.add))
            do(dve.reciprocal(pg, total))
            do(dve.tensor_scalar(total, e12, 1.0, None, ALU.add))
            do(dve.reciprocal(total, total))
            do(dve.tensor_tensor(pair_w[:, :, 0], pg, total, ALU.mult))
            do(dve.tensor_tensor(pair_w[:, :, 1], pair_w[:, :, 0], e12, ALU.mult))
            do(dve.tensor_scalar(rank, rank, -8.0, 40.0, ALU.mult, ALU.add))
            do(dve.tensor_tensor(exp_id[:, 0:2 * NT:2], rank, rank1, ALU.subtract))
            do(dve.tensor_tensor(exp_id[:, 1:2 * NT:2], rank, rank2, ALU.subtract))
            dve.wait_ge(S["count_mm"], after(1))
            before_e = banks[0][:, 0:(NT + 1) * NE].rearrange("p (t e) -> p t e", e=NE)
            tot, ov, ovend, adj_e = before_e[:, NT, :], evec[:, 0, :], evec[:, 1, :], evec[:, 2, :]
            for j in range(2):
                do(dve.tensor_tensor(tmp_e[:, j:2 * NT:2, :], chosen[:, j:2 * NT:2, :], before_e[:, 0:NT, :],
                                     ALU.mult))
            do(dve.tensor_reduce(pos, tmp_e[:, :, :], AX, ALU.add))
            thr = misc[:, THR:THR + 8]
            t8 = tmp_e[:, :, 0:8]
            do(dve.tensor_tensor(t8, along(pos, 8), thr.unsqueeze(1).to_broadcast([P, 2 * NT, 8]), ALU.is_ge))
            do(dve.tensor_reduce(q, t8, AX, ALU.add))
            do(dve.scalar_tensor_tensor(out=rem, in0=q, scalar=-128.0, in1=pos, op0=ALU.mult, op1=ALU.add))
            dve.tensor_tensor(slot_hot[:, :, :], iota.unsqueeze(1).to_broadcast([P, 2 * NT, P]), along(rem, P),
                              ALU.is_equal)
            do(dve.tensor_tensor(wide8[:, :, :], along(tot, 8), thr.unsqueeze(1).to_broadcast([P, NE, 8]), ALU.is_gt))
            do(dve.tensor_reduce(ov, wide8[:, :, :], AX, ALU.add))
            do(dve.tensor_tensor_scan(ovend, misc[:, ONES:ONES + NE], ov, 0.0, ALU.mult, ALU.add))
            do(dve.tensor_tensor(adj_e, ovend, ov, ALU.subtract))
            do(dve.tensor_tensor(adj_e, adj_e, iota[:, 0:NE], ALU.subtract))
            do(dve.tensor_scalar(adj_e, adj_e, NE - 1.0, None, ALU.add))
            do(dve.tensor_tensor(tmp_e[:, :, :], chosen[:, :, :], adj_e.unsqueeze(1).to_broadcast([P, 2 * NT, NE]),
                                 ALU.mult))
            do(dve.tensor_reduce(adj, tmp_e[:, :, :], AX, ALU.add))
            do(dve.tensor_tensor(adj, adj, q, ALU.add))
            do(dve.tensor_scalar(q, q, 1.0, None, ALU.min))
            do(dve.tensor_tensor(adj, adj, q, ALU.mult))
            do(dve.tensor_tensor(blk, exp_id, adj, ALU.add))
            do(dve.scalar_tensor_tensor(out=blk, in0=blk, scalar=1.0, in1=live, op0=ALU.add, op1=ALU.mult))
            hot = planes[:, :, 0:NBLK]
            do(dve.tensor_tensor(hot, iota[:, 1:NBLK + 1].unsqueeze(1).to_broadcast([P, 2 * NT, NBLK]),
                                 along(blk, NBLK), ALU.is_equal))
            dve.tensor_tensor(planes[:, :, NBLK:2 * NBLK], hot, along(misc[:, PAIR:PAIR + 2 * NT], NBLK), ALU.mult)
            dve.tensor_tensor(planes[:, :, 2 * NBLK:3 * NBLK], hot, along(misc[:, TILE:TILE + 2 * NT], NBLK), ALU.mult)\
                .then_inc(S["hot_done"], 1)
            w = tmp_e[:, 0:SPILL, :]
            do(dve.tensor_tensor(w, ovend.unsqueeze(1).to_broadcast([P, SPILL, NE]), along(iota[:, 0:SPILL], NE),
                                 ALU.is_le))
            do(dve.tensor_reduce(evec[:, 3, 0:SPILL], w, AX, ALU.add))
            do(dve.tensor_scalar(spill[:, SPILL:2 * SPILL], evec[:, 3, 0:SPILL], NE - 1.0, None, ALU.min))
            do(dve.tensor_scalar(spill[:, 0:SPILL], iota[:, 0:SPILL], ovend[:, NE - 1:NE], None, ALU.is_lt))
            do(dve.tensor_copy(spill[:, 2 * SPILL:2 * SPILL + 1], ovend[:, NE - 1:NE]))
            dve.wait_ge(S["list_mm"], after(1))
            flat = evec[:, :, :].rearrange("p a e -> p (a e)")
            gap, pair = flat[:, 0:NBLK], flat[:, NBLK:2 * NBLK]
            do(dve.tensor_scalar(gap, banks[2][:, 0:NBLK], -4096.0, 4096.0, ALU.mult, ALU.add))
            do(dve.tensor_scalar(pair, banks[2][:, 2 * NBLK:3 * NBLK], 256.0, None, ALU.mult))
            do(dve.tensor_tensor(pair, pair, banks[2][:, NBLK:2 * NBLK], ALU.add))
            do(dve.tensor_tensor(idx_pair[:, :], gap, pair, ALU.add))
            do(dve.tensor_scalar(idx_tok[:, :], idx_pair[:, :], 1, None, ALU.logical_shift_right))
            dve.sem_inc(S["routed"], 1)

        def stage_c_pool(pool, done):
            steps = Steps(pool, steps_pool, carrier["pool"])

            def step(t, s, start, index):
                steps.round_(start, index, 2 * NEWTON)
                steps.n = s * NEWTON
                pool.wait_ge(S["guess2_done"], after(t + 1))
                carried(pool, "pool")
                newton_rsqrt(steps, pool, small[:, MS + s:MS + s + 1], small[:, RS + s:RS + s + 1],
                             small[:, HALF:HALF + 1], small[:, TMP:TMP + 1]).then_inc(S["rstd2_done"], 1)
                pool.wait_ge(S["h2_done"], after(t + 1))
                carried(pool, "pool")
                if isinstance(t, int) and t == CH:
                    pool.dma_start(h2_d[SEQ:NTOK, :], h2[s][0:NB, :]).then_inc(h2_out[s], 16)
                else:
                    pool.dma_start(h2_d[bass.ds(t * P, P), :], h2[s][:, :]).then_inc(h2_out[s], 16)

            step(0, 0, done, 0)
            step(1, 1, done, 0)
            with pool.Fori(1, CH // 2) as i:
                for s in range(2):
                    step(2 * i + s, s, done, i)
            step(CH, 0, done, CH // 2)
            pool.wait_ge(h2_out[0], 16 * 5)
            pool.wait_ge(h2_out[1], 16 * 4)
            pool.wait_ge(S["x2_done"], after(2 * NT))
            pool.wait_ge(S["t2_mm"], after(2 * NT))
            for s in range(SLOTS):
                pool.memset(xg[s][:, :], 0.0).then_inc(S["gathered_init"], 1)
            pool.wait_ge(S["gathered_init"], after(SLOTS))
            pool.wait_ge(S["routed"], after(1))

            def gather(b, slot, used):
                if not is_first(b, SLOTS):
                    pool.wait_ge(xg_in[slot], 16 * (used - 1))
                    carried(pool, "pool")
                    pool.wait_ge(S["xt2_mm"], after(2 * (b - SLOTS + 1)))
                    carried(pool, "pool")
                pool.tensor_copy(icol[slot][:, :], idx_tok[:, bass.ds(b, 1)]).then_inc(S["icol_done"], 1)
                pool.wait_ge(S["icol_done"], after(b + 1))
                carried(pool, "pool")
                pool.indirect_dma_start(
                    out=xg[slot][:, :], out_offset=None, in_=h2_d,
                    in_offset=bass.IndirectOffsetOnAxis(ap=icol[slot][:, :], axis=0),
                    bounds_check=NTOK - 1, oob_is_err=False).then_inc(xg_in[slot], 16)

            def scatter(b, slot, used, s2):
                if not is_first(b, SLOTS):
                    pool.wait_ge(part_out[slot], 16 * (used - 1))
                    carried(pool, "pool")
                pool.tensor_copy(jcol[slot][:, :], idx_pair[:, bass.ds(b, 1)]).then_inc(S["jcol_done"], 1)
                pool.wait_ge(S["jcol_done"], after(b + 1))
                carried(pool, "pool")
                pool.wait_ge(S["y_ev"], after(2 * b + 2))
                carried(pool, "pool")
                pool.indirect_dma_start(
                    out=part_d, out_offset=bass.IndirectOffsetOnAxis(ap=jcol[slot][:, :], axis=0),
                    in_=yb[s2][:, :], in_offset=None,
                    bounds_check=2 * NTOK - 1, oob_is_err=False).then_inc(part_out[slot], 16)

            for s in range(SLOTS):
                gather(s, s, 1)

            def step_m(b, s, g):
                if not (isinstance(b, int) and b >= NE - 3):
                    gather(b + 3, s % SLOTS, uses(s + 3, g))
                scatter(b, s % SLOTS, uses(s, g), s % 2)

            blocks(pool, step_m)
            for s in range(SLOTS):
                pool.wait_ge(part_out[s], 16 * MAIN_USES[s])

            def more(b, i):
                pool.wait_ge(S["xt2_mm"], after(2 * b))
                carried(pool, "pool")
                gather(b, 0, MAIN_USES[0] + i + 1)
                scatter(b, 0, MAIN_USES[0] + i + 1, 0)
                pool.wait_ge(part_out[0], 16 * (MAIN_USES[0] + i + 1))
                carried(pool, "pool")

            spilled(pool, more)
            pool.sem_inc(S["parts_ready"], 1)

            pool.wait_ge(gfin_in, 16)
            for t in range(NT):
                pool.wait_ge(S["z_done"], after(t + 1))
                pool.tensor_tensor(zt[t % 3][:, :], zt[t % 3][:, :], gfin_b[:, :], ALU.mult)\
                    .then_inc(S["y_done"], 1)

        @block.sync
        def _(sp):
            begin(sp, by_sp)
            for t in range(NT):
                rows = P if t < CH else NB
                src = x_p[t * P:(t + 1) * P, :] if t < CH else x_s
                sp.dma_start(xall[0:rows, t, :], src).then_inc(x_in[t], 16)
                if t == 2:
                    sp.dma_start(gmix_b[:, :], g_mix[0:1, :].to_broadcast([P, D])).then_inc(const_in[0], 16)
                    sp.dma_start(misc[:, :], c_misc).then_inc(const_in[0], 16)
                    for q in range(3):
                        load_piece(sp, q, 0, q)
            for q in range(3, 6):
                load_piece(sp, q, 0, q)
                if q == 5:
                    sp.dma_start(cs[:, :, :], c_cs).then_inc(const_in[1], 16)
                    sp.dma_start(hc[:, :, :], c_hc).then_inc(const_in[1], 16)
                    sp.dma_start(gn_b[:, :], ret_gn[0:1, :].to_broadcast([P, D])).then_inc(const_in[1], 16)
            sp.dma_start(pool_s[0, :, 0:HIST - 1, :], state_pool[0, :, 1:HIST, :]).then_inc(fixed_out, 16)

            def states(d, h, g):
                return d[0, 2 * g:2 * g + 2, bass.ds(h, 1)].rearrange("b a d v -> d (b a) v")

            def store_states(h, g):
                sp.wait_ge(S["s_upd"], after(4 * h + g + 1))
                carried(sp, "sp")
                sp.dma_start(states(ret_s, h, g), sst[g % 2][:, :, :]).then_inc(ss_out[g % 2], 16)

            def load_states(h, g):
                if g >= 2:
                    sp.wait_ge(S["so_mm"], after(4 * h + g - 1))
                    carried(sp, "sp")
                    sp.wait_ge(ss_out[g % 2], 32 * h + 16)
                    carried(sp, "sp")
                sp.dma_start(sst[g % 2][:, :, :], states(state_ret, h, g)).then_inc(ss_in[g % 2], 16)

            def tail(h, between):
                between(0)
                store_states(h, 0)
                between(1)
                store_states(h, 1)
                load_states(h, 2)
                between(2)
                load_states(h, 3)
                between(3)
                store_states(h, 2)
                store_states(h, 3)
                for s, v in ((ss_out[0], 32), (ss_out[1], 32), (st_out, 16), (u_out, 32)):
                    sp.wait_ge(s, v * h + v)
                    carried(sp, "sp")
                sp.sem_inc(S["head_stored"], 1)

            def head(h, first, last):
                if not first:
                    def pieces(i):
                        for q in range(6 + 3 * i, 9 + 3 * i):
                            load_piece(sp, q, h, 18 * h + q)
                    tail(h - 1, pieces)
                    sp.wait_ge(S["o_mm"], after(8 * h))
                    carried(sp, "sp")
                sp.dma_start(hist[0:NB * HIST, :], state_pool[0].rearrange("b r c -> (b r) c")
                             [:, bass.ds(h * P, P)]).then_inc(misc_in, 16)
                if not first:
                    sp.wait_ge(S["wp_ready"], after(h))
                    carried(sp, "sp")
                sp.dma_start(wp_raw[:, :], w_pool[0, bass.ds(h, 1)].rearrange("a c d -> (a c) d"))\
                    .then_inc(misc_in, 16)
                sp.dma_start(ps_b[:, :], pool_scale[0:1, bass.ds(h * DV, DV)].to_broadcast([P, DV]))\
                    .then_inc(misc_in, 16)
                if first:
                    for q in range(6, 18):
                        load_piece(sp, q, h, 18 * h + q)
                if not last:
                    for q in range(6):
                        load_piece(sp, q, h + 1, 18 * (h + 1) + q)
                else:
                    for q in range(6):
                        load_wout(sp, q)
                if not first:
                    sp.wait_ge(S["so_mm"], after(4 * h))
                    carried(sp, "sp")
                for g in range(2):
                    load_states(h, g)
                sp.wait_ge(S["ut_ev"], after(h + 1))
                carried(sp, "sp")
                sp.dma_start(pool_p[0, 0, :, bass.ds(h * P, P)], uout[P - HIST:P, 0, :]).then_inc(u_out, 16)
                sp.dma_start(pool_s[0, :, HIST - 1:HIST, bass.ds(h * P, P)].rearrange("b a c -> (b a) c"),
                             uout[15:P:16, 1, :]).then_inc(u_out, 16)
                sp.wait_ge(S["state_new"], after(8 * h + 8))
                carried(sp, "sp")
                sp.dma_start(ret_p[0, 0, bass.ds(h, 1)].rearrange("a d v -> (a d) v"), state[:, :])\
                    .then_inc(st_out, 16)

            head(0, True, False)
            with sp.Fori(1, H - 1) as h:
                head(h, False, False)
            head(H - 1, False, True)
            tail(H - 1, lambda i: first_loads_c(sp, i))
            sp.wait_ge(fixed_out, 16)
            stage_c_sp(sp)

        def round_piece(act, q, h, n):
            act.wait_ge(raw_in[q % 3], slot_count(h, q))
            _, (hi, _lo), (k, w) = piece(q, 0)
            act.activation(hi, raw[q % 3][:, :].rearrange("p (k n) -> p k n", k=k), ACT.Copy)\
                .then_inc(S["w_hi"], 1)

        @block.scalar
        def _(act):
            begin(act, by_act)
            act.wait_ge(S["zeroed"], after(1))

            def square(t):
                rows = P if t < CH else NB
                act.wait_ge(x_in[t], 16)
                act.wait_ge(S["sq_done"], after(t))
                act.activation(junk_a[0:rows, :], xall[0:rows, t, :], ACT.Square,
                               accum_out=small[0:rows, SS + t:SS + t + 1]).then_inc(S["sq_done"], 1)

            def high_tile(t):
                rows = P if t < CH else NB
                for b in range(2):
                    act.wait_ge(S["xt_mm"], after(2 * t + b + 1))
                    bank = banks[4 + 2 * (t % 2) + b][:, :].rearrange("p (k n) -> p k n", k=4)[:, :, 0:rows]
                    act.activation(hT[0][:, 4 * b:4 * b + 4, t * P:t * P + rows], bank, ACT.Copy)\
                        .then_inc(S["h_hi"], 1)

            for t in range(3):
                square(t)
            for q in range(3):
                round_piece(act, q, 0, q)
            for t in range(3):
                high_tile(t)
                square(3 + t)
            for t in range(6, NT):
                square(t)
            for t in range(3, NT):
                high_tile(t)
                if t < 6:
                    round_piece(act, t, 0, t)

            def head(h, first, last):
                act.wait_ge(S["v_mm"], after(9 * h))
                for n in range(3):
                    for q in range(6 + 3 * n, 9 + 3 * n) if not first else range(6, 9) if n == 2 else ():
                        round_piece(act, q, h, None)
                    act.wait_ge(S["uqk_mm"], after(9 * h + n + 1))
                    if n == 0:
                        act.wait_ge(S["pool_ready"], after(h))
                        act.wait_ge(S["ut_mm"], after(h))
                    bank = banks[n % 2]
                    if n < 2:
                        act.activation(line[0][:, HIST + n * TC:HIST + (n + 1) * TC], bank[:, 0:TC], ACT.Copy)\
                            .then_inc(S["u_ev"], 1)
                    else:
                        act.activation(line[0][:, HIST + 2 * TC:HIST + SEQ], bank[:, 0:TC - NB], ACT.Copy)
                        act.activation(line[0][:, HIST + SEQ + HIST:SPAN:16], bank[:, TC - NB:TC], ACT.Copy)\
                            .then_inc(S["u_ev"], 1)
                for q in range(9 if first else 15, 18):
                    round_piece(act, q, h, None)
                act.wait_ge(S["ht_mm"], after(h + 1))
                tail = line[0][:, HIST + SEQ:SPAN].rearrange("p (b s) -> p b s", s=16)
                act.activation(tail[:, :, 0:HIST], banks[4][:, 0:NB * HIST].rearrange("p (b s) -> p b s", b=NB),
                               ACT.Copy).then_inc(S["hist_ev"], 1)
                act.wait_ge(S["ut_mm"], after(h + 1))
                act.wait_ge(S["head_stored"], after(h))
                act.activation(uout[:, :, :], banks[5][:, 0:2 * P].rearrange("p (a n) -> p a n", a=2), ACT.Copy)\
                    .then_inc(S["ut_ev"], 1)
                act.wait_ge(S["now_ready"], after(h + 1))
                for c in range(NT):
                    lo = 0 if c < CH else Q3
                    act.wait_ge(S["kt_mm"], after(9 * h + c + 1))
                    if c == 0:
                        act.wait_ge(S["kblk_done"], after(h))
                    else:
                        act.wait_ge(S["kv_mm"], after(8 * h + c - 1))
                    act.activation(kz[c % 2][lo:P, :], banks[4][lo:P, 0:P], ACT.Copy if c == CH else ACT.Identity,
                                   scale=P ** -0.5 if c == CH else head_col(0)).then_inc(S["kz_ev"], 1)
                    if 1 <= c <= 6:
                        if c == 1:
                            act.wait_ge(S["uqk_mm"], after(9 * h + 9))
                        if not last:
                            round_piece(act, c - 1, h + 1, None)
                        else:
                            round_wout(act, c - 1)
                    act.wait_ge(S["v_mm"], after(9 * h + c + 1))
                    if c < 2:
                        act.wait_ge(S["so_mm"], after(4 * h))
                    else:
                        act.wait_ge(S["kv_mm"], after(8 * h + c - 1))
                    act.activation(vb[c % 2][:, :], banks[2 + c % 2][:, 0:DV], ACT.Copy).then_inc(S["v_ev"], 1)
                    act.wait_ge(S["on_ready"], after(9 * h + c - 1))
                    act.activation(sg[c % 2][:, :], banks[(9 + c) % 2][:, :], ACT.Sigmoid)\
                        .then_inc(S["sig_done"], 1)

            head(0, True, False)
            with act.Fori(1, H - 1) as h:
                head(h, False, False)
            head(H - 1, False, True)
            stage_c_act(act)

        @block.tensor
        def _(pe):
            begin(pe, by_pe)
            pe.wait_ge(const_in[0], 32)

            def h_over(t):
                rows = P if t < CH else NB
                pe.wait_ge(S["normed"], after(t + 1))
                for b in range(2):
                    pe.wait_ge(S["h_lo"], after(2 * (t - 2) + b + 1))
                    for j in range(4):
                        k = 4 * b + j
                        mm = pe.transpose(banks[4 + 2 * (t % 2) + b][:, j * P:j * P + rows],
                                          xall[0:rows, t, k * P:(k + 1) * P], ident[0:rows, 0:rows])
                    mm.then_inc(S["xt_mm"], 1)

            def attend_samples(h, n):
                def grow(g):
                    pe.wait_ge(S["s_upd"], after(4 * h + g - 1))
                    for i in range(2):
                        mm = pe.matmul(banks[2 + g % 2][:, i * DV:(i + 1) * DV], kblk[Q3:P, 2 * g + i, :],
                                       vb[0][Q3:P, :], start=True, stop=True)
                    mm.then_inc(S["skv_mm"], 1)

                def read(g):
                    pe.wait_ge(S["s_upd"], after(4 * h + g + 1))
                    for i in range(2):
                        b = 2 * g + i
                        mm = pe.matmul(banks[6][Q3:P, 0:DV], qm[:, b, :], sst[g % 2][:, i, :],
                                       start=(b == 0), stop=(b == NB - 1))
                    mm.then_inc(S["so_mm"], 1)

                if n == 0:
                    pe.wait_ge(S["kblk_done"], after(h + 1))
                    pe.wait_ge(S["v_ev"], after(9 * h + 9))
                    pe.wait_ge(S["qm_done"], after(h + 1))
                    grow(0)
                    grow(1)
                elif n <= 4:
                    if n == 1:
                        pe.wait_ge(S["o_used"], after(9 * h + 8))
                        pe.matmul(banks[6][Q3:P, DV:2 * DV], ps32[:, :], wp[:, :], start=True, stop=True)
                    read(n - 1)
                    if n <= 2:
                        grow(n + 1)

            def head(h, first):
                for n in range(9):
                    j, tc = n // 3, n % 3
                    if first and n < 3:
                        for t in range(3 * n, 3 * n + 3):
                            h_over(t)
                        pe.wait_ge(S["h_lo"], after(6 * (n + 1)))
                    elif not first:
                        attend_samples(h - 1, n)
                    if n < 2:
                        pe.wait_ge(S["sig_done"], after(9 * h))
                    elif n < 5:
                        pe.wait_ge(S["u_ev"], after(3 * h + n - 1))
                    else:
                        pe.wait_ge(S["qk_ev"], after(6 * h + n - 4))
                    if tc == 0:
                        pe.wait_ge(S["w_lo"], after(18 * h + 2 * (j + 1)))
                    out = banks[n % 2][:, 0:TC]
                    for k in range(KT):
                        mm = three(pe, out, [w[:, j, k, :] for w in wuqk],
                                   [x[:, k, tc * TC:(tc + 1) * TC] for x in hT], k == 0, k == KT - 1)
                    mm.then_inc(S["uqk_mm"], 1)
                    if n == 5:
                        pe.wait_ge(misc_in, 48 * h + 48)
                        pe.wait_ge(S["kz_ev"], after(9 * h))
                        pe.transpose(banks[4][:, 0:NB * HIST], hist[0:NB * HIST, :],
                                     ident[0:NB * HIST, 0:NB * HIST]).then_inc(S["ht_mm"], 1)
                pe.wait_ge(S["hist_ev"], after(h + 1))
                pe.wait_ge(S["u_ev"], after(3 * h + 3))
                pe.wait_ge(S["scm_done"], after(8 * h))
                pe.transpose(banks[5][:, 0:P], line[0][:, HIST + SEQ - P:HIST + SEQ], ident)
                pe.transpose(banks[5][:, P:2 * P], line[0][:, HIST + SEQ:SPAN], ident).then_inc(S["ut_mm"], 1)

                def before(c):
                    pe.wait_ge(S["kz_ev"], after(9 * h + c))
                    at = c * P if c < CH else LAST
                    pe.transpose(banks[4][:, 0:P], kT[:, at:at + P], ident).then_inc(S["kt_mm"], 1)
                    if c == CH:
                        return
                    if c == 0:
                        pe.wait_ge(S["ut_ev"], after(h + 1))
                        pe.wait_ge(S["qk_ev"], after(6 * h + 6))
                    pe.wait_ge(S["scm_done"], after(8 * h + c))
                    pe.matmul(banks[5][:, 0:P], kT[:, at:at + P], qT[:, at:at + P], start=True, stop=True)\
                        .then_inc(S["sc_mm"], 1)

                def project(c):
                    if c == 0:
                        pe.wait_ge(S["w_lo"], after(18 * h + 18))
                    if c >= 2:
                        pe.wait_ge(S["sig_done"], after(9 * h + c - 1))
                        pe.wait_ge(S["v_ev"], after(9 * h + c - 1))
                    else:
                        pe.wait_ge(S["s_upd"], after(4 * h))
                        pe.wait_ge(S["qk_ev"], after(6 * h + 5 + c))
                    at = c * P if c < CH else LAST
                    gates, v = banks[(9 + c) % 2], banks[2 + c % 2]
                    gates = gates[:, :].rearrange("p (a n) -> p a n", a=2)
                    for k in range(KT):
                        x = [t[:, k, at:at + P] for t in hT]
                        for xi, wi in ((0, 0), (0, 1), (1, 0)):
                            first, last = k == 0 and xi + wi == 0, k == KT - 1 and xi == 1
                            g = pe.matmul(gates, x[xi], wvg[wi][:, 1:3, k, :], start=first, stop=last)
                            m = pe.matmul(v[:, 0:DV], x[xi], wvg[wi][:, 0, k, :], start=first, stop=last)
                    g.then_inc(S["g_mm"], 1)
                    m.then_inc(S["v_mm"], 1)

                def attend(c):
                    s = c % 2
                    pe.wait_ge(S["o_used"], after(9 * h + c))
                    pe.wait_ge(S["pool_ready"], after(h + 1))
                    pe.matmul(banks[6][:, DV:2 * DV], line[1][:, HIST + c * P:HIST + (c + 1) * P], wp[:, :],
                              start=True, stop=True)
                    pe.wait_ge(S["scm_done"], after(8 * h + c + 1))
                    pe.wait_ge(S["v_ev"], after(9 * h + c + 1))
                    o = pe.matmul(banks[6][:, 0:DV], scm[s][:, :], vb[s][:, :], start=True, stop=(c == 0))
                    if c > 0:
                        pe.wait_ge(S["qx_done"], after(7 * h + c))
                        pe.wait_ge(S["state_new"], after(8 * h + c))
                        o = pe.matmul(banks[6][:, 0:DV], qx[s][:, :], state[:, :], start=False, stop=True)
                    o.then_inc(S["o_mm"], 1)
                    pe.wait_ge(S["kz_ev"], after(9 * h + c + 1))
                    pe.wait_ge(S["state_new"], after(8 * h + c))
                    pe.matmul(banks[7][:, 0:DV], kz[s][:, :], vb[s][:, :], start=True, stop=True)\
                        .then_inc(S["kv_mm"], 1)

                for c in range(NT):
                    if c == 0:
                        project(0)
                    before(c)
                    if c > 0:
                        project(c)
                    if c > 0:
                        attend(c - 1)

            head(0, True)
            with pe.Fori(1, H) as h:
                head(h, False)
            stage_c_pe(pe, lambda n: attend_samples(H - 1, n))

        def low_piece(dve, q):
            _, (hi, lo), (k, w) = piece(q, 0)
            dve.tensor_tensor(lo, raw[q % 3][:, :].rearrange("p (k n) -> p k n", k=k), hi, ALU.subtract)\
                .then_inc(S["w_lo"], 1)

        @block.vector
        def _(dve):
            begin(dve, by_dve)
            steps = Steps(dve, steps_dve)
            steps.do(dve.memset(line[0][:, 0:HIST], 0.0))
            steps.do(dve.memset(ps32[:, :], 0.0))
            steps.do(dve.memset(small[:, :], 1.0))
            dve.sem_inc(S["zeroed"], 1)

            def rms_guess(a, b):
                dve.wait_ge(S["sq_done"], after(b))
                ms, rs = small[:, MS + a:MS + b], small[:, RS + a:RS + b]
                steps.do(dve.tensor_scalar(ms, small[:, SS + a:SS + b], 1.0 / D, EPS, ALU.mult, ALU.add))
                return ms, rs, rsqrt_guess(steps, dve, ms, rs, bits[:, a:b])

            def rms(a, b):
                ms, rs, last = rms_guess(a, b)
                steps.do(last)
                steps.do(newton_rsqrt(steps, dve, ms, rs, small[:, HX + a:HX + b], small[:, TX + a:TX + b]))

            def normalise(t):
                rows = P if t < CH else NB
                dve.scalar_tensor_tensor(out=xall[0:rows, t, :], in0=xall[0:rows, t, :],
                                         scalar=small[0:rows, RS + t:RS + t + 1], in1=gmix_b[0:rows, :],
                                         op0=ALU.mult, op1=ALU.mult).then_inc(S["normed"], 1)

            def low_tile(t):
                rows = P if t < CH else NB
                for b in range(2):
                    dve.wait_ge(S["h_hi"], after(2 * t + b + 1))
                    at = (slice(None), slice(4 * b, 4 * b + 4), slice(t * P, t * P + rows))
                    bank = banks[4 + 2 * (t % 2) + b][:, :].rearrange("p (k n) -> p k n", k=4)[:, :, 0:rows]
                    dve.tensor_tensor(hT[1][at], bank, hT[0][at], ALU.subtract).then_inc(S["h_lo"], 1)

            rms(0, 3)
            dve.wait_ge(const_in[0], 32)
            for t in range(3):
                normalise(t)
            for q in range(3):
                dve.wait_ge(S["w_hi"], after(q + 1))
                low_piece(dve, q)
            for t in range(3):
                low_tile(t)
            rms(3, 6)
            for t in range(3, 6):
                normalise(t)
            rms_guess(6, NT)[2].then_inc(S["rms_guessed"], 1)
            for t in range(3, 6):
                low_tile(t)
            dve.wait_ge(S["rms_ready"], after(1))
            for t in range(6, NT):
                normalise(t)
            for t in range(6, NT):
                dve.wait_ge(S["w_hi"], after(t - 2))
                low_piece(dve, t - 3)
                low_tile(t)
            dve.wait_ge(const_in[1], 48)
            before_heads = steps.n
            per_head, per_tail = 48, 4

            def finish(h, c):
                r = slice(0 if c < CH else Q3, P)
                s = c % 2
                if c < CH:
                    dve.wait_ge(S["o_mm"], after(8 * h + c + 1))
                else:
                    dve.wait_ge(S["so_mm"], after(4 * h + 4))
                dve.wait_ge(S["sig_done"], after(9 * h + c + 1))
                dve.wait_ge(S["sum_done"], after(9 * h + c))
                o = banks[6][r, 0:DV]
                dve.tensor_tensor(pgate[r, :], banks[6][r, DV:2 * DV], sg[s][r, 0:DV], ALU.mult)\
                    .then_inc(S["pg_ready"], 1)
                steps.do(dve.bn_stats(small[r, STAT:STAT + 6], o))
                carried(dve, "dve")
                steps.do(dve.bn_aggr(small[r, MEAN:MEAN + 2], small[r, STAT:STAT + 6]))
                steps.do(dve.tensor_scalar(small[r, VAR:VAR + 1], small[r, VAR:VAR + 1], EPS, None, ALU.add))
                rsqrt_guess(steps, dve, small[r, VAR:VAR + 1], small[r, GUESS:GUESS + 1], bits[r, 9:10])\
                    .then_inc(S["guess_done"], 1)

            def finish_rest(h, c):
                r = slice(0 if c < CH else Q3, P)
                s = c % 2
                o = banks[6][r, 0:DV]
                dve.wait_ge(S["rstd_done"], after(9 * h + c + 1))
                dve.tensor_scalar(onorm[r, :], o, small[r, MEAN:MEAN + 1], small[r, GUESS:GUESS + 1],
                                  ALU.subtract, ALU.mult).then_inc(S["o_used"], 1)
                dve.wait_ge(S["o_used"], after(9 * h + c + 1))
                dve.wait_ge(S["sgn_done"], after(9 * h + c + 1))
                dve.tensor_tensor(onorm[r, :], onorm[r, :], sgn[s][r], ALU.mult).then_inc(S["on_ready"], 1)

            def tail(h, between):
                n = steps.n
                for g in range(4):
                    dve.wait_ge(S["skv_mm"], after(4 * h + g + 1))
                    dve.wait_ge(ss_in[g % 2], 32 * h + 16 * (g // 2) + 16)
                    dve.scalar_tensor_tensor(
                        out=sst[g % 2][:, :, :], in0=sst[g % 2][:, :, :], scalar=head_col(2),
                        in1=banks[2 + g % 2][:, :].rearrange("p (a n) -> p a n", a=2), op0=ALU.mult, op1=ALU.add)\
                        .then_inc(S["s_upd"], 1)
                    between(g)
                finish(h, CH)
                assert steps.n - n == per_tail, steps.n - n

            def head(h, first, last):
                steps.round_(before_heads - per_tail, h, per_head)
                if first:
                    steps.n = per_tail
                else:
                    def lows(g):
                        for q in range(6 + 3 * g, 9 + 3 * g):
                            dve.wait_ge(S["w_hi"], after(18 * h + q + 1))
                            low_piece(dve, q)
                    tail(h - 1, lows)
                dve.wait_ge(S["kz_ev"], after(9 * h))
                dve.wait_ge(S["s_upd"], after(4 * h))
                dve.tensor_copy(small[:, NOW:NOW + 8], head_tab(h, HC0, 8)).then_inc(S["now_ready"], 1)
                for n in range(3, 9):
                    dve.wait_ge(S["uqk_mm"], after(9 * h + n + 1))
                    dve.wait_ge(S["qk_ev"], after(6 * h + n - 3))
                    bank, dst = banks[n % 2], (qT, kT)[(n - 3) // 3]
                    at = slice((n % 3) * TC, (n % 3 + 1) * TC)
                    dve.tensor_tensor(dst[:, at], bank[:, 0:TC], cs[:, 0, at], ALU.mult)
                    dve.tensor_tensor(rot[0:64, :], bank[64:P, 0:TC], cs[64:P, 1, at], ALU.mult)
                    steps.do(dve.tensor_tensor(rot[64:P, :], bank[0:64, 0:TC], cs[0:64, 1, at], ALU.mult))
                    dve.tensor_tensor(dst[:, at], dst[:, at], rot[:, :], ALU.add).then_inc(S["qk_ev"], 1)
                    if first:
                        for q in range(2 * n, 2 * n + 2):
                            dve.wait_ge(S["w_hi"], after(q + 1))
                            low_piece(dve, q)
                    elif n == 3:
                        finish_rest(h - 1, CH)
                dve.wait_ge(misc_in, 48 * h + 48)
                dve.tensor_tensor(wp[:, :], wp_raw[:, :], ps_b[:, :], ALU.mult).then_inc(S["wp_ready"], 1)

                def scores(c):
                    dve.wait_ge(S["sc_mm"], after(8 * h + c + 1))
                    if c > 1:
                        dve.wait_ge(S["o_mm"], after(8 * h + c - 1))
                    dve.tensor_tensor(scm[c % 2][:, :], banks[5][:, 0:P], head_tab(h, 0, P), ALU.mult)\
                        .then_inc(S["scm_done"], 1)
                    if c > 0:
                        dve.tensor_tensor(qx[c % 2][:, :], qT[:, c * P:(c + 1) * P], head_tab(h, P, P), ALU.mult)\
                            .then_inc(S["qx_done"], 1)

                def pool_means():
                    dve.wait_ge(S["u_ev"], after(3 * h + 3))
                    dve.wait_ge(S["hist_ev"], after(h + 1))
                    u, a, b = line[0], line[1], line[2]
                    steps.do(dve.tensor_tensor(a[:, 1:SPAN], u[:, 1:SPAN], u[:, 0:SPAN - 1], ALU.add))
                    for level, (src, dst, lo, gap) in enumerate(((a, b, 3, 2), (b, a, 7, 4), (a, b, 15, 8))):
                        steps.do(dve.scalar_tensor_tensor(
                            out=dst[:, lo:SPAN], in0=src[:, lo - gap:SPAN - gap], scalar=head_col(4 + level),
                            in1=src[:, lo:SPAN], op0=ALU.mult, op1=ALU.add))
                    steps.do(dve.tensor_tensor(b[:, HIST:HIST + 16], b[:, HIST:HIST + 16],
                                               head_tab(h, 2 * P, 16), ALU.mult))
                    steps.do(dve.scalar_tensor_tensor(
                        out=a[:, HIST:SPAN], in0=b[:, HIST:SPAN], scalar=head_col(3), in1=u[:, HIST:SPAN],
                        op0=ALU.mult, op1=ALU.subtract))
                    dve.tensor_copy(ps32[:, 24:32], a[:, HIST + SEQ + HIST:SPAN:16]).then_inc(S["pool_ready"], 1)

                def grow_state(c):
                    dve.wait_ge(S["kv_mm"], after(8 * h + c + 1))
                    if c == 0:
                        dve.wait_ge(S["head_stored"], after(h))
                        ins = dve.tensor_copy(state[:, :], banks[7][:, 0:DV])
                    else:
                        dve.wait_ge(S["state_new"], after(8 * h + c))
                        ins = dve.scalar_tensor_tensor(out=state[:, :], in0=state[:, :], scalar=head_col(1),
                                                       in1=banks[7][:, 0:DV], op0=ALU.mult, op1=ALU.add)
                    ins.then_inc(S["state_new"], 1)

                for c in range(NT):
                    if c == 0:
                        pool_means()
                    if c < CH:
                        scores(c)
                    if 1 <= c <= 6:
                        dve.wait_ge(S["w_hi"], after(18 * (h + 1) + c))
                        if not last:
                            low_piece(dve, c - 1)
                        else:
                            low_wout(dve, c - 1)
                    if c == CH:
                        dve.wait_ge(S["kz_ev"], after(9 * h + 9))
                        dve.tensor_tensor(kblk[Q3:P, :, :], kz[0][Q3:P, :].unsqueeze(1).to_broadcast([P - Q3, NB, P]),
                                          misc[Q3:P, KMASK:KMASK + NB].unsqueeze(2).to_broadcast([P - Q3, NB, P]),
                                          ALU.mult).then_inc(S["kblk_done"], 1)
                        dve.tensor_tensor(qm[:, :, :], qT[:, SEQ:NTOK].unsqueeze(2).to_broadcast([P, NB, 32]),
                                          misc[:, QMASK:QMASK + NB * 32].rearrange("p (b j) -> p b j", b=NB),
                                          ALU.mult).then_inc(S["qm_done"], 1)
                    if c > 0:
                        grow_state(c - 1)
                        finish(h, c - 1)
                        finish_rest(h, c - 1)
                assert steps.n == per_head, steps.n

            head(0, True, False)
            with dve.Fori(1, H - 1) as h:
                head(h, False, False)
            head(H - 1, False, True)
            steps.round_(before_heads - per_tail, H, per_head)

            def lows(g):
                low_wout_rest(dve, g)
                if g == 3:
                    low_mixed(dve, 0, 0)
            tail(H - 1, lows)
            finish_rest(H - 1, CH)
            stage_c_dve(dve, before_heads + H * per_head)

        @block.gpsimd
        def _(pool):
            begin(pool, by_pool)
            steps = Steps(pool, steps_pool, carrier["pool"])
            pool.wait_ge(S["rms_guessed"], after(1))
            newton_rsqrt(steps, pool, *(small[:, a + 6:a + NT] for a in (MS, RS, HX, TX)))\
                .then_inc(S["rms_ready"], 1)
            pool.wait_ge(const_in[1], 48)
            per_head = 9 * NEWTON

            def head(h):
                steps.round_(NEWTON, h, per_head)
                for c in range(NT + 1):
                    if c < NT:
                        s = c % 2
                        pool.wait_ge(S["sig_done"], after(9 * h + c + 1))
                        carried(pool, "pool")
                        pool.tensor_tensor(sgn[s], sgn[s], gn_b[:, bass.ds(h * DV, DV)],
                                           ALU.mult).then_inc(S["sgn_done"], 1)
                    if c == 0:
                        continue
                    c1 = c - 1
                    s = c1 % 2
                    pool.wait_ge(S["guess_done"], after(9 * h + c1 + 1))
                    carried(pool, "pool")
                    newton_rsqrt(steps, pool, small[:, VAR:VAR + 1], small[:, GUESS:GUESS + 1],
                                 small[:, HALF:HALF + 1], small[:, TMP:TMP + 1]).then_inc(S["rstd_done"], 1)
                    pool.wait_ge(S["on_ready"], after(9 * h + c1 + 1))
                    carried(pool, "pool")
                    if c1 >= 2:
                        pool.wait_ge(mix_out[s], 16 * ((5 - s) * h + (c1 - 2) // 2 + 1))
                        carried(pool, "pool")
                    pool.tensor_tensor(mixed[s][:, :], onorm[:, :], pgate[:, :], ALU.add).then_inc(S["sum_done"], 1)
                    pool.wait_ge(S["sum_done"], after(9 * h + c1 + 1))
                    carried(pool, "pool")
                    if c1 < CH:
                        dst, src = mixed_d[c1 * P:(c1 + 1) * P, bass.ds(h * DV, DV)], mixed[s][:, :]
                    else:
                        dst, src = mixed_d[SEQ:NTOK, bass.ds(h * DV, DV)], mixed[s][120:P, :]
                    pool.dma_start(dst, src).then_inc(mix_out[s], 16)
                for s in range(2):
                    pool.wait_ge(mix_out[s], 16 * (5 - s) * (h + 1))
                    carried(pool, "pool")
                assert steps.n == per_head

            with pool.Fori(0, H) as h:
                head(h)
            stage_c_pool(pool, NEWTON + H * per_head)


_INS = ['x_prompt', 'x_sample', 'state_pool', 'state_ret', 'g_mix', 'w_in', 'w_pool', 'pool_scale', 'ret_gn',
        'w_out', 'g_ffn', 'w_grp', 'w_exp', 'w1', 'w3', 'w2', 'g_final']
_OUTS = [(1, SEQ, D), (NB, 1, D), (1, 1, HIST, 512), (1, 1, H, P, DV), (1, NB, HIST, 512), (1, NB, H, P, DV)]


def kernel(**inputs):
    import numpy as _np
    import concourse.bacc as _bacc
    from concourse import mybir as _mybir
    from concourse.bass_utils import run_bass_kernel_spmd as _run

    nc = _bacc.Bacc("TRN2", target_bir_lowering=False, num_devices=1)
    arrays, args = {}, []
    for name in _INS:
        arrays[f"in_{name}_dram"] = _np.ascontiguousarray(inputs[name])
    for name, table in zip(("tables", "head_tables", "masks"), shape_constants()):
        arrays[f"const_{name}_dram"] = table
    for name, a in arrays.items():
        args.append(nc.dram_tensor(name, a.shape, _mybir.dt.from_np(a.dtype), kind="ExternalInput").ap())
    for i, shape in enumerate(_OUTS):
        args.append(nc.dram_tensor(f"out_{i}_dram", shape, _mybir.dt.float32, kind="ExternalOutput").ap())
    step_kernel(nc, *args)
    r = _run(nc, [arrays], core_ids=[0])
    return tuple(r.results[0][f"out_{i}_dram"] for i in range(len(_OUTS)))
```
